# Optimizing a Trainium2 kernel written in Bass

```python
import math
import jax
import jax.numpy as jnp
from jax import lax
import numpy as np

D_MODEL = 1024
BATCH = 1
SEQ = 512
DEPTH = 2
DEC_BATCH = 8
DEC_SEQ = 1
PAST_LEN = 2048
PAGE_SIZE = 128

N_META = 16
N_MIXERS = 2
N_ATTN_LAYERS = (DEPTH + 1) // 2
N_SSD_LAYERS = DEPTH // 2
N_HEADS = 16
HEAD_DIM = D_MODEL // N_HEADS
N_KV_HEADS = 4
N_IDX_HEADS = 8
IDX_DIM = 64
TOPK_MAX = 256
Q_BLOCK = 128
Q_DIM = N_HEADS * HEAD_DIM
KV_DIM = N_KV_HEADS * HEAD_DIM
QI_DIM = N_IDX_HEADS * IDX_DIM
ATTN_IN_DIM = Q_DIM + 2 * KV_DIM + QI_DIM + IDX_DIM + N_IDX_HEADS
D_INNER = 2 * D_MODEL
SSD_HEAD_DIM = 64
SSD_HEADS = D_INNER // SSD_HEAD_DIM
SSD_GROUPS = 4
HEADS_PER_GROUP = SSD_HEADS // SSD_GROUPS
D_STATE = 128
CONV_W = 4
CONV_DIM = D_INNER + 2 * SSD_GROUPS * D_STATE
SSD_IN_DIM = D_INNER + CONV_DIM + SSD_HEADS
CHUNK = 128
FFN_HIDDEN = 2816
EPS = 1e-6

kernel_name = 'dsa_ssd_macaron_meta_hybrid_step'

def rms_norm(x, g):
    xf = x.astype(jnp.float32)
    y = xf * lax.rsqrt(jnp.mean(xf * xf, axis=-1, keepdims=True) + EPS)
    return (y * g.astype(jnp.float32)).astype(x.dtype)

def swiglu_ffn(x, g, w_in, w_out):
    h = rms_norm(x, g) @ w_in
    a, b = jnp.split(h, 2, axis=-1)
    return (jax.nn.silu(a) * b) @ w_out

def attn_project(x, g, w_in, q_norm, k_norm, kidx_norm):
    B, L = x.shape[:2]
    h = rms_norm(x, g) @ w_in
    splits = [Q_DIM, Q_DIM + KV_DIM, Q_DIM + 2 * KV_DIM, Q_DIM + 2 * KV_DIM + QI_DIM,
              Q_DIM + 2 * KV_DIM + QI_DIM + IDX_DIM]
    q, k, v, qi, ki, wi = jnp.split(h, splits, axis=-1)
    q = rms_norm(q.reshape(B, L, N_HEADS, HEAD_DIM), q_norm)
    k = rms_norm(k.reshape(B, L, N_KV_HEADS, HEAD_DIM), k_norm)
    v = v.reshape(B, L, N_KV_HEADS, HEAD_DIM)
    qi = qi.reshape(B, L, N_IDX_HEADS, IDX_DIM)
    ki = rms_norm(ki, kidx_norm)
    wi = wi * (N_IDX_HEADS ** -0.5)
    return q, k, v, qi, ki, wi

def indexer_scores(qi, wi, ki, q_pos, k_pos):
    dots = jnp.einsum('bqhd,bld->bqhl', qi, ki).astype(jnp.float32) * (IDX_DIM ** -0.5)
    s = jnp.einsum('bqh,bqhl->bql', wi.astype(jnp.float32), jax.nn.relu(dots))
    return jnp.where(k_pos[None, None, :] <= q_pos[:, :, None], s, -jnp.inf)

def sparse_attend(q, k_sel, v_sel, valid):
    B, Q = q.shape[:2]
    qg = q.reshape(B, Q, N_KV_HEADS, N_HEADS // N_KV_HEADS, HEAD_DIM)
    s = jnp.einsum('bqgrd,bqkgd->bqgrk', qg, k_sel).astype(jnp.float32) * (HEAD_DIM ** -0.5)
    s = jnp.where(valid[:, :, None, None, :], s, -jnp.inf)
    p = jax.nn.softmax(s, axis=-1).astype(v_sel.dtype)
    o = jnp.einsum('bqgrk,bqkgd->bqgrd', p, v_sel)
    return o.reshape(B, Q, Q_DIM)

def dsa_prompt(q, k, v, qi, ki, wi, topk):
    B, T = q.shape[:2]
    n_blk = -(-T // Q_BLOCK)
    pad = n_blk * Q_BLOCK - T

    def blocks(a):
        a = jnp.pad(a, [(0, 0), (0, pad)] + [(0, 0)] * (a.ndim - 2))
        return a.reshape((B, n_blk, Q_BLOCK) + a.shape[2:]).swapaxes(0, 1)

    k_pos = jnp.arange(T)
    q_pos = jnp.arange(n_blk * Q_BLOCK).reshape(n_blk, Q_BLOCK)

    def one_block(args):
        qb, qib, wib, pos = args
        sc = indexer_scores(qib, wib, ki, pos[None], k_pos)
        _, idx = lax.top_k(sc, topk)
        k_sel = jax.vmap(lambda kb, ib: kb[ib])(k, idx)
        v_sel = jax.vmap(lambda vb, ib: vb[ib])(v, idx)
        return sparse_attend(qb, k_sel, v_sel, idx <= pos[None, :, None])

    o = lax.map(one_block, (blocks(q), blocks(qi), blocks(wi), q_pos))
    return o.swapaxes(0, 1).reshape(B, n_blk * Q_BLOCK, Q_DIM)[:, :T]

def dsa_sample(q, k_new, v_new, qi, ki_new, wi, cache_k, cache_v, cache_kidx, page_table, topk):
    B, S = q.shape[:2]
    ki_past = cache_kidx[page_table].reshape(B, PAST_LEN, IDX_DIM)
    ki_all = jnp.concatenate([ki_past, ki_new.astype(ki_past.dtype)], axis=1)
    k_pos = jnp.arange(PAST_LEN + S)
    q_pos = PAST_LEN + jnp.arange(S)
    sc = indexer_scores(qi, wi, ki_all, q_pos[None], k_pos)
    _, idx = lax.top_k(sc, topk)
    is_new = idx >= PAST_LEN
    pidx = jnp.minimum(idx, PAST_LEN - 1)
    phys = jax.vmap(lambda pt, i: pt[i])(page_table, pidx // PAGE_SIZE)
    off = pidx % PAGE_SIZE
    nidx = jnp.clip(idx - PAST_LEN, 0, S - 1)

    def select(cache, new):
        past = cache[phys, off]
        cur = jax.vmap(lambda nb, ib: nb[ib])(new.astype(past.dtype), nidx)
        return jnp.where(is_new[..., None, None], cur, past)

    return sparse_attend(q, select(cache_k, k_new), select(cache_v, v_new), idx <= q_pos[None, :, None])

def causal_conv(xbc, conv_state, w, b):
    L = xbc.shape[1]
    xp = jnp.concatenate([conv_state.astype(xbc.dtype), xbc], axis=1)
    y = sum(xp[:, j:j + L] * w[j] for j in range(CONV_W)) + b
    return jax.nn.silu(y), xp[:, -(CONV_W - 1):]

def ssd_chunked(x, dt, a, bm, cm, h0, chunk):
    B, L = x.shape[:2]
    c = L // chunk
    G, Hg, P, N = SSD_GROUPS, HEADS_PER_GROUP, SSD_HEAD_DIM, D_STATE
    xr = (x.astype(jnp.float32) * dt[..., None]).reshape(B, c, chunk, G, Hg, P)
    br = bm.astype(jnp.float32).reshape(B, c, chunk, G, N)
    cr = cm.astype(jnp.float32).reshape(B, c, chunk, G, N)
    a_cum = jnp.cumsum((dt * a).reshape(B, c, chunk, G, Hg), axis=2)
    seg = a_cum[:, :, :, None] - a_cum[:, :, None, :]
    causal = jnp.tril(jnp.ones((chunk, chunk), dtype=bool))[None, None, :, :, None, None]
    decay = jnp.exp(jnp.where(causal, seg, -jnp.inf))
    cb = jnp.einsum('bclgn,bcsgn->bclsg', cr, br)
    y_diag = jnp.einsum('bclsg,bclsgh,bcsghp->bclghp', cb, decay, xr)
    decay_s = jnp.exp(a_cum[:, :, -1:] - a_cum)
    states = jnp.einsum('bcsgn,bcsgh,bcsghp->bcghpn', br, decay_s, xr)
    chunk_decay = jnp.exp(a_cum[:, :, -1])

    def step(h, inp):
        st, dec = inp
        return dec[..., None, None] * h + st, h

    h_final, h_prev = lax.scan(step, h0.reshape(B, G, Hg, P, N),
                               (states.swapaxes(0, 1), chunk_decay.swapaxes(0, 1)))
    h_prev = h_prev.swapaxes(0, 1)
    y_off = jnp.einsum('bclgn,bcghpn,bclgh->bclghp', cr, h_prev, jnp.exp(a_cum))
    y = (y_diag + y_off).reshape(B, L, SSD_HEADS, P)
    return y, h_final.reshape(B, SSD_HEADS, P, N)

def ssd_mixer(x, g, w_in, conv_w, conv_b, dt_bias, a_log, d_skip, gate_norm, w_out,
              conv_state, h0, segments):
    B, L = x.shape[:2]
    h = rms_norm(x, g) @ w_in
    z, xbc, dt_raw = jnp.split(h, [D_INNER, D_INNER + CONV_DIM], axis=-1)
    xbc, new_conv = causal_conv(xbc, conv_state, conv_w, conv_b)
    xh, bm, cm = jnp.split(xbc, [D_INNER, D_INNER + SSD_GROUPS * D_STATE], axis=-1)
    xh = xh.reshape(B, L, SSD_HEADS, SSD_HEAD_DIM)
    bm = bm.reshape(B, L, SSD_GROUPS, D_STATE)
    cm = cm.reshape(B, L, SSD_GROUPS, D_STATE)
    dt = jax.nn.softplus(dt_raw.astype(jnp.float32) + dt_bias.astype(jnp.float32))
    a = -jnp.exp(a_log.astype(jnp.float32))
    state = h0.astype(jnp.float32)
    ys = []
    for start, length, chunk in segments:
        sl = slice(start, start + length)
        y_seg, state = ssd_chunked(xh[:, sl], dt[:, sl], a, bm[:, sl], cm[:, sl], state, chunk)
        ys.append(y_seg)
    y = jnp.concatenate(ys, axis=1)
    y = y + d_skip.astype(jnp.float32)[:, None] * xh.astype(jnp.float32)
    y = y.reshape(B, L, D_INNER) * jax.nn.silu(z.astype(jnp.float32))
    y = rms_norm(y.reshape(B, L, SSD_GROUPS, D_INNER // SSD_GROUPS),
                 gate_norm.reshape(SSD_GROUPS, D_INNER // SSD_GROUPS)).reshape(B, L, D_INNER)
    return y.astype(x.dtype) @ w_out, state, new_conv

def setup_inputs(seed: int = 0) -> dict:
    key = jax.random.key(seed)
    ks = jax.random.split(key, 40)
    f32 = jnp.float32

    def nrm(k, shape, fan_in):
        return jax.random.normal(k, shape, f32) * (fan_in ** -0.5)

    def gain(k, shape):
        return 1.0 + 0.05 * jax.random.normal(k, shape, f32)

    n_pages = PAST_LEN // PAGE_SIZE
    n_used = DEC_BATCH * n_pages
    n_pool = n_used + n_used // 4 + 1
    page_table = jax.random.permutation(ks[0], n_pool)[:n_used].reshape(DEC_BATCH, n_pages).astype(jnp.int32)
    dt0 = jnp.exp(jax.random.uniform(ks[1], (N_SSD_LAYERS, SSD_HEADS), f32, math.log(1e-3), math.log(1e-1)))
    dt_bias = dt0 + jnp.log(-jnp.expm1(-dt0))
    a_log = jnp.log(jax.random.uniform(ks[2], (N_SSD_LAYERS, SSD_HEADS), f32, 1.0, 16.0))
    return {
        'x_prompt': jax.random.normal(ks[3], (BATCH, SEQ, D_MODEL), f32),
        'x_sample': jax.random.normal(ks[4], (DEC_BATCH, DEC_SEQ, D_MODEL), f32),
        'cache_k': jax.random.normal(ks[5], (N_ATTN_LAYERS, n_pool, PAGE_SIZE, N_KV_HEADS, HEAD_DIM), f32),
        'cache_v': jax.random.normal(ks[6], (N_ATTN_LAYERS, n_pool, PAGE_SIZE, N_KV_HEADS, HEAD_DIM), f32),
        'cache_kidx': jax.random.normal(ks[7], (N_ATTN_LAYERS, n_pool, PAGE_SIZE, IDX_DIM), f32),
        'page_table': page_table,
        'state_ssm': 0.1 * jax.random.normal(ks[8], (N_SSD_LAYERS, DEC_BATCH, SSD_HEADS, SSD_HEAD_DIM, D_STATE), f32),
        'state_conv': jax.random.normal(ks[9], (N_SSD_LAYERS, DEC_BATCH, CONV_W - 1, CONV_DIM), f32),
        'meta_tokens': jax.random.normal(ks[10], (N_META, D_MODEL), f32),
        'norm_ffn_a': gain(ks[11], (DEPTH, D_MODEL)),
        'w_ffn_a_in': nrm(ks[12], (DEPTH, D_MODEL, 2 * FFN_HIDDEN), D_MODEL),
        'w_ffn_a_out': nrm(ks[13], (DEPTH, FFN_HIDDEN, D_MODEL), FFN_HIDDEN),
        'norm_mix': gain(ks[14], (DEPTH, D_MODEL)),
        'norm_ffn_b': gain(ks[15], (DEPTH, D_MODEL)),
        'w_ffn_b_in': nrm(ks[16], (DEPTH, D_MODEL, 2 * FFN_HIDDEN), D_MODEL),
        'w_ffn_b_out': nrm(ks[17], (DEPTH, FFN_HIDDEN, D_MODEL), FFN_HIDDEN),
        'w_attn_in': nrm(ks[18], (N_ATTN_LAYERS, D_MODEL, ATTN_IN_DIM), D_MODEL),
        'q_norm': gain(ks[19], (N_ATTN_LAYERS, HEAD_DIM)),
        'k_norm': gain(ks[20], (N_ATTN_LAYERS, HEAD_DIM)),
        'kidx_norm': gain(ks[21], (N_ATTN_LAYERS, IDX_DIM)),
        'w_attn_out': nrm(ks[22], (N_ATTN_LAYERS, Q_DIM, D_MODEL), Q_DIM),
        'w_ssd_in': nrm(ks[23], (N_SSD_LAYERS, D_MODEL, SSD_IN_DIM), D_MODEL),
        'conv_w': nrm(ks[24], (N_SSD_LAYERS, CONV_W, CONV_DIM), CONV_W),
        'conv_b': 0.01 * jax.random.normal(ks[25], (N_SSD_LAYERS, CONV_DIM), f32),
        'dt_bias': dt_bias,
        'a_log': a_log,
        'd_skip': gain(ks[26], (N_SSD_LAYERS, SSD_HEADS)),
        'gate_norm': gain(ks[27], (N_SSD_LAYERS, D_INNER)),
        'w_ssd_out': nrm(ks[28], (N_SSD_LAYERS, D_INNER, D_MODEL), D_INNER),
    }

def reference(x_prompt, x_sample, cache_k, cache_v, cache_kidx, page_table, state_ssm, state_conv,
              meta_tokens, norm_ffn_a, w_ffn_a_in, w_ffn_a_out, norm_mix, norm_ffn_b, w_ffn_b_in, w_ffn_b_out,
              w_attn_in, q_norm, k_norm, kidx_norm, w_attn_out,
              w_ssd_in, conv_w, conv_b, dt_bias, a_log, d_skip, gate_norm, w_ssd_out):
    B = x_prompt.shape[0]
    meta = jnp.broadcast_to(meta_tokens.astype(x_prompt.dtype)[None], (B, N_META, D_MODEL))
    xp = jnp.concatenate([meta, x_prompt], axis=1)
    xs = x_sample
    topk_p = min(TOPK_MAX, SEQ // 4)
    topk_s = min(TOPK_MAX, (PAST_LEN + DEC_SEQ) // 4)
    kp_l, vp_l, kip_l, ks_l, vs_l, kis_l = [], [], [], [], [], []
    hp_l, cp_l, hs_l, cs_l = [], [], [], []
    for i in range(DEPTH):
        xp = xp + 0.5 * swiglu_ffn(xp, norm_ffn_a[i], w_ffn_a_in[i], w_ffn_a_out[i])
        xs = xs + 0.5 * swiglu_ffn(xs, norm_ffn_a[i], w_ffn_a_in[i], w_ffn_a_out[i])
        j = i // N_MIXERS
        if i % N_MIXERS == 0:
            ap = (w_attn_in[j], q_norm[j], k_norm[j], kidx_norm[j])
            qp, kp, vp, qip, kip, wip = attn_project(xp, norm_mix[i], *ap)
            xp = xp + dsa_prompt(qp, kp, vp, qip, kip, wip, topk_p) @ w_attn_out[j]
            qs, ksn, vsn, qis, kis, wis = attn_project(xs, norm_mix[i], *ap)
            xs = xs + dsa_sample(qs, ksn, vsn, qis, kis, wis, cache_k[j], cache_v[j], cache_kidx[j],
                                 page_table, topk_s) @ w_attn_out[j]
            kp_l.append(kp)
            vp_l.append(vp)
            kip_l.append(kip)
            ks_l.append(ksn)
            vs_l.append(vsn)
            kis_l.append(kis)
        else:
            sp = (w_ssd_in[j], conv_w[j], conv_b[j], dt_bias[j], a_log[j], d_skip[j], gate_norm[j], w_ssd_out[j])
            conv0 = jnp.zeros((B, CONV_W - 1, CONV_DIM), xp.dtype)
            h0 = jnp.zeros((B, SSD_HEADS, SSD_HEAD_DIM, D_STATE), jnp.float32)
            yp, hp, cp = ssd_mixer(xp, norm_mix[i], *sp, conv0, h0,
                                   ((0, N_META, N_META), (N_META, SEQ, CHUNK)))
            xp = xp + yp
            ys, hs, cs = ssd_mixer(xs, norm_mix[i], *sp, state_conv[j], state_ssm[j],
                                   ((0, DEC_SEQ, DEC_SEQ),))
            xs = xs + ys
            hp_l.append(hp)
            cp_l.append(cp)
            hs_l.append(hs)
            cs_l.append(cs)
        xp = xp + 0.5 * swiglu_ffn(xp, norm_ffn_b[i], w_ffn_b_in[i], w_ffn_b_out[i])
        xs = xs + 0.5 * swiglu_ffn(xs, norm_ffn_b[i], w_ffn_b_in[i], w_ffn_b_out[i])
    y_prompt = xp[:, N_META:]
    y_sample = xs
    new_k_prompt = jnp.stack(kp_l)
    new_v_prompt = jnp.stack(vp_l)
    new_kidx_prompt = jnp.stack(kip_l)
    new_k_sample = jnp.stack(ks_l)
    new_v_sample = jnp.stack(vs_l)
    new_kidx_sample = jnp.stack(kis_l)
    new_ssm_prompt = jnp.stack(hp_l)
    new_conv_prompt = jnp.stack(cp_l)
    new_ssm_sample = jnp.stack(hs_l)
    new_conv_sample = jnp.stack(cs_l)
    return (y_prompt, y_sample, new_k_prompt, new_v_prompt, new_kidx_prompt,
            new_k_sample, new_v_sample, new_kidx_sample,
            new_ssm_prompt, new_conv_prompt, new_ssm_sample, new_conv_sample)


_drawn_inputs = setup_inputs


def setup_inputs(seed=0):
    import zlib

    import numpy as np

    out = dict(_drawn_inputs(seed))
    spreads = {}
    factors = {'q_norm': 5.287, 'conv_b': 3.34, 'd_skip': 2.783}
    for name, (base, spread) in spreads.items():
        noise = np.random.default_rng([zlib.crc32(name.encode()), seed]).standard_normal(out[name].shape)
        drawn = base * np.exp(spread * noise) if base else spread * noise
        out[name] = jnp.asarray(drawn.astype(out[name].dtype))
    for name, factor in factors.items():
        out[name] = (out[name] * factor).astype(out[name].dtype)
    return out
```

```python
from contextlib import ExitStack

import numpy as np

import concourse.bass as bass
from concourse import mybir

F32 = mybir.dt.float32
F32R = mybir.dt.float32r
BF16 = mybir.dt.bfloat16
I32 = mybir.dt.int32
U32 = mybir.dt.uint32
ALU = mybir.AluOpType
ACT = mybir.ActivationFunctionType
AX = mybir.AxisListType
ds = bass.ds

P = 128
D = 1024
DT = D // P
META, SEQ, S = 16, 512, 8
T = META + SEQ
N = T + S
H = N // 2
FFN = 2816
FT = FFN // P
GROUPS = (12, 10)
NH, NKV, REP, HD = 16, 4, 4, 64
NIH = 8
QT, KT2, VT2, QIT = 8, 2, 2, 4
K0, V0, QI0, KI0 = 8, 10, 12, 16
AT = 17
PAST, PAGE = 2048, 128
NPG = PAST // PAGE
TOPK_P, TOPK_S = 128, 256
NORMED = [KI0, K0, K0 + 1] + list(range(QT))
PICK = 2 * (len(NORMED) - 1)
HROWS = 2 * len(NORMED)
DI = 2048
ZT, XT, BT, CT = 16, 16, 4, 4
CVT = XT + BT + CT
SH, SG = 32, 4
EPS = 1e-6
BIG = 1e30
GONE = -3e38
POOL = 161
BLK = 16
CREDIT = 2

SECTIONS = []
def _section(name, count):
    SECTIONS.append((name, sum(c for _, _, c in SECTIONS), count))
def _ffn_sections(f):
    for g, kt in enumerate(GROUPS):
        _section(f"in{f}{g}", kt)
        _section(f"out{f}{g}", DT)
_ffn_sections(0)
_section("attn_in", 9)
_section("attn_out", 4)
_ffn_sections(1)
_ffn_sections(2)
_section("ssd_in", 21)
_section("ssd_out", 8)
_ffn_sections(3)
BASE = {name: base for name, base, _ in SECTIONS}
COUNT = {name: count for name, _, count in SECTIONS}
CHUNKS = sum(COUNT.values())
GBASE = {(f, g): f * FT + sum(GROUPS[:g]) for f in range(4) for g in range(2)}
NORM = {"ffn0": 0, "attn": 1, "ffn1": 2, "ffn2": 3, "ssd": 4, "ffn3": 5}


class Chain:

    def __init__(self, eng, sem):
        self.eng, self.sem, self.n, self.at = eng, sem, 0, 0

    def link(self, ins):
        ins.then_inc(self.sem, 1)
        self.n += 1
        self.eng.wait_ge(self.sem, self.n + self.at)

    def mark(self, ins):
        ins.then_inc(self.sem, 1)
        self.n += 1
        return self.n

    def after(self, n):
        self.eng.wait_ge(self.sem, n)

    def loop(self, i, per):
        self.at = i * per
        self.start, self.per = self.n, per

    def end(self, rounds):
        assert self.n - self.start == self.per, (self.n - self.start, self.per)
        self.n = self.start + self.per * rounds
        self.at = 0


def build(nc, I, O, upto=99):
    ctx = ExitStack()

    def sb(name, shape, dt=F32, where=None):
        return (where or ctx).enter_context(nc.sbuf_tensor(name, shape, dt))

    def sem(name):
        return ctx.enter_context(nc.semaphore(name))

    acc = ctx.enter_context(nc.psum_tensor("acc", [P, 8, 512], F32))

    xT = sb("xT", [P, DT, N])
    raw = sb("raw", [P, 2, BLK * P])
    wh, wl = sb("wh", [P, 2, BLK * P], F32R), sb("wl", [P, 2, BLK * P], F32R)
    scr = sb("scr", [P, 4, N])
    silu_a, hid = scr[:, 0:2], scr[:, 2:4]
    sq, ssum, rstd = sb("sq", [P, N]), sb("ssum", [P, N]), sb("rstd", [P, N])
    gains = sb("gains", [P, 6, DT])
    ones = sb("ones", [P, P])
    epsc = sb("epsc", [P, 1])
    pages = sb("pages", [P, S * NPG], I32)
    vrow = sb("vrow", [P, S], I32)
    lane = sb("lane", [P, 2], I32)
    credit = sb("credit", [P, 4])

    w_loaded = [sem("w_loaded0"), sem("w_loaded1")]
    wh_ready, wl_ready = sem("wh_ready"), sem("wl_ready")
    chunk_done = sem("chunk_done")
    epilogue_done = sem("epilogue_done")
    silu_ready, g_ready = sem("silu_ready"), sem("g_ready")
    x_loaded, const_ready, consts_loaded = sem("x_loaded"), sem("const_ready"), sem("consts_loaded")
    ssum_ready, norm_sum_done, std_ready = sem("ssum_ready"), sem("norm_sum_done"), sem("std_ready")
    xn_ready, xh_ready, xl_ready = sem("xn_ready"), sem("xh_ready"), sem("xl_ready")
    dve_chain, pool_chain, act_chain = sem("dve_chain"), sem("pool_chain"), sem("act_chain")
    out_done = sem("out_done")


    ident, negm = sb("ident", [P, P]), sb("negm", [P, P])
    pick = sb("pick", [P, 2 * PICK + 2])
    fused = sb("fused", [P, P])
    swap = sb("swap", [P, P])
    ones_b, before_b = sb("ones_b", [P, P], BF16), sb("before_b", [P, P], BF16)
    headg = sb("headg", [P, 4])

    upto1 = sb("upto1", [P, P])

    core_ctx = ExitStack()
    bias = sb("bias", [P, 4, T], F32, core_ctx)
    neg_s = sb("neg_s", [P, 2, T], F32, core_ctx)
    prob = sb("prob", [P, 2, T], F32, core_ctx)
    probT = sb("probT", [P, 2, 4 * P + 16], F32, core_ctx)
    Ss = sb("Ss", [P, S, NPG + 1, NH], F32, core_ctx)
    orow = sb("orow", [P, D], F32, core_ctx)
    core_ctx.close()
    x_ctx = ExitStack()
    xh, xl = sb("xh", [P, DT, N], F32R, x_ctx), sb("xl", [P, DT, N], F32R, x_ctx)

    ffn_ctx = ExitStack()
    gh = sb("gh", [P, max(GROUPS), N], F32R, ffn_ctx)
    gl = sb("gl", [P, max(GROUPS), N], F32R, ffn_ctx)
    ffn_ctx.close()


    att_ctx = ExitStack()
    hT = sb("hT", [P, AT, N], F32, att_ctx)
    kid = sb("kid", [P, N], F32, att_ctx)
    vtok = sb("vtok", [P, 5, NKV * HD], F32, att_ctx)
    wtok = sb("wtok", [P, 5, NIH], F32, att_ctx)
    krow = sb("krow", [P, S * NPG], I32, att_ctx)
    vnew = sb("vnew", [1, S, NKV * HD], F32, att_ctx)
    qis = sb("qis", [P, S, NIH], F32, att_ctx)
    wsel = sb("wsel", [24, S, NIH], F32, att_ctx)
    wib = sb("wib", [P, S, NIH], F32, att_ctx)
    qblk = sb("qblk", [P, S, 2, NIH], F32, att_ctx)
    rowmin, rsum, rinv = sb("rowmin", [P, 2], F32, att_ctx), sb("rsum", [P, NH], F32, att_ctx), sb("rinv", [P, NH], F32, att_ctx)
    top8 = sb("top8", [P, NIH], F32, att_ctx)
    scs = sb("scs", [P, S, NPG + 1], F32, att_ctx)
    keys, kmask = sb("keys", [P, S, NPG + 1], I32, att_ctx), sb("kmask", [P, S, NPG + 1], I32, att_ctx)
    khi, klo = sb("khi", [P, S, NPG + 1], F32, att_ctx), sb("klo", [P, S, NPG + 1], F32, att_ctx)
    rank = sb("rank", [P, S, NPG + 1], F32, att_ctx)
    tie_b = sb("tie_b", [P, S], BF16, att_ctx)
    cnt_b = sb("cnt_b", [P, S], BF16, att_ctx)
    cand, step = sb("cand", [P, S], F32, att_ctx), sb("step", [P, S], F32, att_ctx)
    smax, srinv = sb("smax", [P, P], F32, att_ctx), sb("srinv", [P, S, NH], F32, att_ctx)
    srow, sdiag = sb("srow", [P, 1], F32, att_ctx), sb("sdiag", [P, P], F32, att_ctx)
    kic = sb("kic", [P, S // 2, NPG, PAGE], F32, att_ctx)
    kv = kic[:].rearrange("p a b c -> p (a b c)").rearrange("p (q c) -> p q c", q=2)
    att_ctx.close()

    ssd_ctx = ExitStack()
    zT = sb("zT", [P, ZT, N], F32, ssd_ctx)
    xbc = sb("xbc", [P, CVT, N], F32, ssd_ctx)
    convw, convb = sb("convw", [P, CVT, 4], F32, ssd_ctx), sb("convb", [P, CVT], F32, ssd_ctx)
    window = sb("window", [P, CVT, S, 4], F32, ssd_ctx)
    tail = sb("tail", [P, CVT, 3], F32, ssd_ctx)
    featp = sb("featp", [P, 2, XT], F32, ssd_ctx)
    headp = sb("headp", [P, 2, SH], F32, ssd_ctx)
    dtok, dA = sb("dtok", [P, 5, SH], F32, ssd_ctx), sb("dA", [P, 5, SH], F32, ssd_ctx)
    decay, cum = sb("decay", [P, SH], F32, ssd_ctx), sb("cum", [P, 2, SH], F32, ssd_ctx)
    cdecay = sb("cdecay", [P, SH], F32, ssd_ctx)
    ssd_ctx.close()
    y_ctx = ExitStack()
    yl = sb("yl", [P, XT, N], F32R, y_ctx)
    y_ctx.close()
    x_ctx.close()
    scan_ctx = ExitStack()
    hst = sb("hst", [P, SH, HD], F32, scan_ctx)
    xr, xd = sb("xr", [P, SH, HD], F32, scan_ctx), sb("xd", [P, SH, HD], F32, scan_ctx)
    Et = sb("Et", [P, 2, 4, P], F32, scan_ctx)
    Ct = sb("Ct", [P, 2, 4, P], F32, scan_ctx)
    scan_ctx.close()
    step_ctx = ExitStack()
    hs = sb("hs", [P, 2, XT, P], F32, step_ctx)
    hp = sb("hp", [P, 2, XT, P], F32, step_ctx)
    step_ctx.close()
    yh_ctx = ExitStack()
    yh = sb("yh", [P, XT, N], F32R, yh_ctx)
    yh_ctx.close()


    def halves(ap):
        return ap.rearrange("p (h n) -> p h n", h=2)

    def pair(slot, t=0):
        return acc[:, slot * 4 + 2 * t:slot * 4 + 2 * t + 2, 0:H]

    def chunks(eng, count, body, chain=None, per=0):
        if count // 2:
            with eng.Fori(0, count // 2) as i:
                if chain:
                    chain.loop(i, 2 * per)
                for u in range(2):
                    body(i * 2, u)
                if chain:
                    chain.end(count // 2)
        if count % 2:
            if chain:
                chain.loop(0, per)
            body(0, count - 1)
            if chain:
                chain.end(1)

    def sp_stream(sp, section, source, width, start=0, beside=None, between=None):
        base, count = BASE[section], COUNT[section]

        def load(i, u, wait=True):
            slot = (base + u) % 2
            if wait:
                sp.wait_ge(wl_ready, i + (base + u - 1))
            src = source[ds(i + (start + u), 1)].rearrange("a p c -> p (a c)")
            sp.dma_start(raw[:, slot, 0:width], src).then_inc(w_loaded[slot], 16)

        if base == 0:
            load(0, 0, False)
            load(0, 1, False)
            with sp.Fori(1, count // 2) as i:
                for u in range(2):
                    load(i * 2, u)
                beside(i - 1)
        elif beside:
            with sp.Fori(0, count // 2) as i:
                for u in range(2):
                    load(i * 2, u)
                beside(i)
        elif between:
            load(0, 0)
            load(0, 1)
            between()
            with sp.Fori(1, count // 2) as i:
                for u in range(2):
                    load(i * 2, u)
            if count % 2:
                load(0, count - 1)
        else:
            chunks(sp, count, load)

    def act_round(act, base, i, u):
        n, slot = base + u, (base + u) % 2
        act.wait_ge(chunk_done, i + (n + 1))
        act.wait_ge(w_loaded[slot], 8 * i + 16 * (n // 2 + 1))
        nc.scalar.activation(wh[:, slot], raw[:, slot], ACT.Copy).then_inc(wh_ready, 1)

    def act_norm(act, k):
        act.wait_ge(norm_sum_done, k + 1)
        slot = norm_slot_of(k)
        nc.scalar.activation(halves(rstd[:]), pair(slot), ACT.Sqrt, bias=epsc[:, 0:1],
                             scale=1.0 / D).then_inc(std_ready, 1)
        for t in range(DT):
            act.wait_ge(xn_ready, DT * k + t + 1)
            nc.scalar.activation(xh[:, t], scr[:, t % 4], ACT.Copy).then_inc(xh_ready, 1)

    def act_ffn_in(act, f, g):
        base = BASE[f"in{f}{g}"]

        def body(i, u):
            n, slot = base + u, (base + u) % 2
            act_round(act, base + 1, i, u)
            act.wait_ge(epilogue_done, i + (n + 1))
            act.wait_ge(chunk_done, i + (n + 1 + CREDIT))
            nc.scalar.activation(halves(silu_a[:, slot]), pair(slot), ACT.Silu).then_inc(silu_ready, 1)

        chunks(act, COUNT[f"in{f}{g}"], body)

    def act_rounds(act, section, ahead=True):
        count = COUNT[section] - (0 if ahead else 1)
        chunks(act, count, lambda i, u: act_round(act, BASE[section] + 1, i, u))

    def dve_rest(dve, base, i, u):
        n, slot = base + u, (base + u) % 2
        dve.wait_ge(wh_ready, i + (n + 1))
        nc.vector.tensor_tensor(wl[:, slot], raw[:, slot], wh[:, slot].bitcast(F32),
                                ALU.subtract).then_inc(wl_ready, 1)

    def dve_norm(dve, chain, k):
        dve.wait_ge(std_ready, k + 1)
        chain.link(nc.vector.reciprocal(rstd[:], rstd[:]))
        for t in range(DT):
            if t >= 4:
                dve.wait_ge(xl_ready, DT * k + t - 3)
            nc.vector.scalar_tensor_tensor(scr[:, t % 4], xT[:, t], gains[:, k, t:t + 1], rstd[:],
                                           ALU.mult, ALU.mult).then_inc(xn_ready, 1)

    def dve_ffn_in(dve, f, g):
        base, gb = BASE[f"in{f}{g}"], GBASE[f, g]

        def body(i, u):
            n, slot = base + u, (base + u) % 2
            dve_rest(dve, base + 1, i, u)
            dve.wait_ge(g_ready, i + (gb + u + 1))
            dve.wait_ge(silu_ready, i + (gb + u + 1))
            nc.vector.tensor_tensor(halves(hid[:, slot]), halves(silu_a[:, slot]), pair(slot, 1),
                                    ALU.mult).then_inc(epilogue_done, 1)

        chunks(dve, COUNT[f"in{f}{g}"], body)

    def dve_residual(dve, section, scale, tiles=1, ahead=True):
        base, count = BASE[section], COUNT[section]

        def body(i, u, ahead=True):
            n, slot = base + u, (base + u) % 2
            if ahead:
                dve_rest(dve, base + 1, i, u)
            dve.wait_ge(epilogue_done, i + (n + CREDIT))
            dve.wait_ge(chunk_done, i + (n + 1 + CREDIT))
            x = xT[:, ds(i * tiles + u * tiles, tiles)].rearrange("p t (h n) -> p (t h) n", h=2)
            a = acc[:, slot * 4:slot * 4 + 2 * tiles, 0:H]
            nc.vector.scalar_tensor_tensor(x, a, scale, x, ALU.mult, ALU.add).then_inc(epilogue_done, 1)

        if ahead:
            chunks(dve, count, body)
        else:
            with dve.Fori(0, count // 2 - 1) as i:
                body(i * 2, 0)
                body(i * 2, 1)
            body(count - 2, 0)
            body(count - 2, 1, False)

    def dve_copy_out(dve, section, dst, count, first=0, tiles=2):
        base = BASE[section] + first

        def body(i, u):
            n, slot = base + u, (base + u) % 2
            dve_rest(dve, base + 1, i, u)
            dve.wait_ge(chunk_done, i + (n + 1 + CREDIT))
            out = dst[:, ds(i * 2 + (first + u) * 2, tiles)].rearrange("p t (h n) -> p (t h) n", h=2)
            nc.vector.tensor_scalar(out, acc[:, slot * 4:slot * 4 + 2 * tiles, 0:H], 1.0, None, ALU.mult
                                    ).then_inc(epilogue_done, 1)

        chunks(dve, count, body)

    def pool_sumsq(pool, chain, k, section=None, tiles=1):
        for t in range(DT):
            if section is not None:
                pool.wait_ge(epilogue_done, BASE[section] + t // tiles + 1 + CREDIT)
            elif t == 0:
                pool.wait_ge(x_loaded, 16)
            if t == 0:
                if k:
                    pool.wait_ge(norm_sum_done, k)
                chain.link(nc.gpsimd.tensor_tensor(ssum[:], xT[:, t], xT[:, t], ALU.mult))
                continue
            chain.link(nc.gpsimd.tensor_tensor(sq[:], xT[:, t], xT[:, t], ALU.mult))
            ins = nc.gpsimd.tensor_tensor(ssum[:], ssum[:], sq[:], ALU.add)
            if t == DT - 1:
                ins.then_inc(ssum_ready, 1)
            else:
                chain.link(ins)

    def pool_norm(pool, k):
        for t in range(DT):
            pool.wait_ge(xh_ready, DT * k + t + 1)
            nc.gpsimd.tensor_tensor(xl[:, t], scr[:, t % 4], xh[:, t].bitcast(F32),
                                    ALU.subtract).then_inc(xl_ready, 1)

    def pool_ffn_in(pool, chain, f, g):
        base, gb, count = BASE[f"in{f}{g}"], GBASE[f, g], COUNT[f"in{f}{g}"]

        def body(i, u):
            slot = (base + u) % 2
            pool.wait_ge(epilogue_done, i + (base + u + 1 + CREDIT))
            h = gh[:, ds(i + u, 1)].rearrange("p a n -> p (a n)")
            l = gl[:, ds(i + u, 1)].rearrange("p a n -> p (a n)")
            chain.link(nc.gpsimd.tensor_tensor(h, hid[:, slot], ones[:, 0:1].broadcast_to([P, N]), ALU.mult))
            nc.gpsimd.tensor_tensor(l, hid[:, slot], h.bitcast(F32), ALU.subtract).then_inc(g_ready, 1)

        chunks(pool, count, body, chain, 1)

    def norm_slot(k):
        first = [BASE["in00"], BASE["attn_in"], BASE["in10"], BASE["in20"], BASE["ssd_in"], BASE["in30"]][k]
        return first % 2, first

    def norm_slot_of(k):
        return norm_slot(k)[0]

    def pe_norm(pe, k):
        slot, first = norm_slot(k)
        pe.wait_ge(ssum_ready, k + 1)
        pe.wait_ge(epilogue_done, first + 1)
        for h in range(2):
            mm = nc.tensor.matmul(acc[:, slot * 4 + h, 0:H], ones[:], ssum[:, h * H:(h + 1) * H],
                                  start=True, stop=True)
        mm.then_inc(norm_sum_done, 1)

    def pe_pairs(pe, section, ready, first=0, count=None, tiles=2):
        base = BASE[section] + first

        def body(i, u):
            n, slot = base + u, (base + u) % 2
            pe.wait_ge(epilogue_done, i + (n + 1))
            pe.wait_ge(wl_ready, i + (n + 1))
            for kt in range(DT):
                ready(kt)
                for t in range(tiles):
                    c = (kt * 2 + t) * P
                    for w, x in ((wh, xh), (wh, xl), (wl, xh)):
                        for h in range(2):
                            mm = nc.tensor.matmul(acc[:, slot * 4 + 2 * t + h, 0:H], w[:, slot, c:c + P],
                                                  x[:, kt, h * H:(h + 1) * H],
                                                  start=(kt == 0 and w is wh and x is xh),
                                                  stop=(kt == DT - 1 and w is wl))
            mm.then_inc(chunk_done, 1)

        chunks(pe, COUNT[section] if count is None else count, body)

    def pe_singles(pe, section, kts, rh, rl, ready):
        base = BASE[section]

        def body(i, u):
            n, slot = base + u, (base + u) % 2
            pe.wait_ge(epilogue_done, i + (n + 1))
            pe.wait_ge(wl_ready, i + (n + 1))
            for kt in range(kts):
                ready(kt)
                for w, xlow in ((wh, False), (wh, True), (wl, False)):
                    for h in range(2):
                        x = (rl if xlow else rh)(kt)[:, h * H:(h + 1) * H]
                        mm = nc.tensor.matmul(acc[:, slot * 4 + h, 0:H], w[:, slot, kt * P:(kt + 1) * P], x,
                                              start=(kt == 0 and w is wh and not xlow),
                                              stop=(kt == kts - 1 and w is wl))
            mm.then_inc(chunk_done, 1)

        chunks(pe, COUNT[section], body)

    def pe_ffn(pe, f, k):
        pe_norm(pe, k)
        for g, kts in enumerate(GROUPS):
            pe_pairs(pe, f"in{f}{g}", lambda kt: pe.wait_ge(xl_ready, DT * k + kt + 1))
            pe_singles(pe, f"out{f}{g}", kts, lambda kt: gh[:, kt], lambda kt: gl[:, kt],
                       lambda kt: pe.wait_ge(g_ready, GBASE[f, g] + kt + 1 + CREDIT))

    def ffn_norm_k(f):
        return NORM[f"ffn{f}"]

    kic_loaded, att_in_done = sem("kic_loaded"), sem("att_in_done")
    sp_keys_loaded = [sem("sp_keys_loaded0"), sem("sp_keys_loaded1")]
    pool_loaded = [sem("pool_loaded0"), sem("pool_loaded1")]
    kv_used = sem("kv_used")
    rows_ready = sem("rows_ready")
    consts = sem("consts")
    headsq, headsum, headstd = sem("headsq"), sem("headsum"), sem("headstd")
    turned, turned_copied = sem("turned"), sem("turned_copied")
    dots_done, relu_done, wsum_done = sem("dots_done"), sem("relu_done"), sem("wsum_done")
    sdots_done, sdots_read = sem("sdots_done"), sem("sdots_read")
    count_asked, count_done = sem("count_asked"), sem("count_done")
    sscore_done, sscore_copied = sem("sscore_done"), sem("sscore_copied")
    bias_ready, sside = sem("bias_ready"), sem("sside")
    qk_done, neg_ready, exp_done = sem("qk_done"), sem("neg_ready"), sem("exp_done")
    pt_done, pt_ready = sem("pt_done"), [sem("pt_ready0"), sem("pt_ready1")]
    pv_done, orow_ready, ot_done, ot_copied = sem("pv_done"), sem("orow_ready"), sem("ot_done"), sem("ot_copied")
    spv_done, so_ready = sem("spv_done"), sem("so_ready")
    at_xh, at_xl = sem("at_xh"), sem("at_xl")
    sexp_asked, sexp_done = sem("sexp_asked"), sem("sexp_done")
    dve_side = sem("dve_side")

    headrinv, headspread, headread = sem("headrinv"), sem("headspread"), sem("headread")
    spread_ready = sem("spread_ready")
    SPREADS = [0, 1, "kid"] + list(range(2, len(NORMED)))
    spread = bias[:].rearrange("p a n -> p (a n)")[0:HROWS, 0:HROWS * HD]
    QTILES = [(j, min(P, T - j * P), min(P * (j + 1), T)) for j in range(5)]
    SKEYS = NPG + 1

    def wide(j, ap, m, w):
        return ap[0:m, 0:2, 0:w // 2] if w > 512 else ap[0:m, 0:1, 0:w]

    def flat(j, ap, m, w):
        return ap[0:m, 0:w].rearrange("p (a n) -> p a n", a=2 if w > 512 else 1)

    def page_of(eng, s, g):
        return eng.value_load(pages[0:1, ds(s * NPG + g, 1)], min_val=0, max_val=POOL - 1)

    def sp_index_pages(sp, g):
        for s in range(S):
            pg = page_of(sp, s, g)
            half = (s % 2) * HD
            dst = kic[half:half + HD, s // 2, ds(g, 1), :].rearrange("p a c -> p (a c)")
            src = I["kidx"][ds(pg, 1)].rearrange("a p c -> p (a c)")
            sp.dma_start(dst, src).then_inc(kic_loaded, 16)

    def sp_keys(sp):
        with sp.Fori(0, S // 2) as i:
            for q in range(2):
                for g in range(NPG // 2):
                    pg = page_of(sp, i * 2 + q, g)
                    if g == 0:
                        sp.wait_ge(kv_used, i * 2 + (q + 1))
                    sp.dma_start(kv[:, q, g * 256:(g + 1) * 256],
                                 I["kpages"][ds(pg, 1)].rearrange("a p c -> p (a c)")).then_inc(sp_keys_loaded[q], 16)

    def pool_keys_values(pool):
        pool.wait_ge(rows_ready, 2)
        krows = I["kpages"].rearrange("a p c -> (a p) c")
        vrows = I["vpages"].rearrange("a (q r) c -> (a q) (r c)", q=8)
        for s in range(S):
            pool.wait_ge(kv_used, s + 1)
            for g in range(NPG // 2, NPG):
                n = s * NPG + g
                nc.gpsimd.indirect_dma_start(kv[:, s % 2, g * 256:(g + 1) * 256], None, krows,
                                             bass.IndirectOffsetOnAxis(krow[:, n:n + 1], 0)).then_inc(pool_loaded[s % 2], 16)
        for s in range(S):
            pool.wait_ge(kv_used, S + s + 1)
            nc.gpsimd.indirect_dma_start(kv[:, s % 2], None, vrows,
                                         bass.IndirectOffsetOnAxis(vrow[:, s:s + 1], 0)).then_inc(pool_loaded[s % 2], 16)

    def pe_attention(pe):
        pe.wait_ge(epilogue_done, BASE["attn_out"] + CREDIT)
        for s in range(S):
            for t in range(VT2):
                c = s * 256 + t * P
                mm = nc.tensor.matmul(acc[0:1, c // 512, c % 512:c % 512 + P], hT[:, V0 + t, T + s:T + s + 1], ident[:],
                                      start=True, stop=True)
        mm.then_inc(turned, 1)
        for j, m, _ in QTILES:
            m = m + S if j == 4 else m
            for t in range(VT2):
                nc.tensor.transpose(acc[0:m, 4 + j // 2, (j % 2) * 256 + t * P:(j % 2) * 256 + (t + 1) * P],
                                    hT[:, V0 + t, j * P:j * P + m], ident[:])
            nc.tensor.transpose(acc[0:m, 7, j * NIH:(j + 1) * NIH],
                                hT[HD:HD + NIH, KI0, j * P:j * P + m],
                                ident[HD:HD + NIH, HD:HD + NIH])
        mm = nc.tensor.matmul(acc[:, 7, 64:96], swap[:], hT[:, QI0:QI0 + QIT, T:N], start=True, stop=True)
        mm.then_inc(turned, 1)
        pe.wait_ge(turned_copied, 1)
        for n, t in enumerate(NORMED):
            pe.wait_ge(headsq, n + 1)
            w = pick[:, PICK - 2 * n:PICK - 2 * n + HROWS]
            for h in range(2):
                mm = nc.tensor.matmul(acc[0:HROWS, h, 0:H], w, scr[:, n % 4, h * H:(h + 1) * H],
                                      start=(n == 0), stop=(n == len(NORMED) - 1))
            mm.then_inc(headsum, 1)
        pe.wait_ge(turned_copied, 5)
        mm = nc.tensor.matmul(acc[:, 7, 128:192], ones[0:24, :], wsel[:].rearrange("p s h -> p (s h)"), start=True, stop=True)
        mm.then_inc(turned, 1)
        kicf = kic[:].rearrange("p s g c -> p s (g c)")

        def cached_dots(s):
            half = (s % 2) * HD
            for g in range(NPG):
                c = (s // 2) * P + g * NIH
                mm = nc.tensor.matmul(acc[:, 4 + s % 2, c:c + NIH], kicf[half:half + HD, s // 2, g::NPG],
                                      qis[half:half + HD, s, :], start=True, stop=True)
            mm.then_inc(sdots_done, 1)

        pe.wait_ge(kic_loaded, 16 * S * NPG)
        for s in range(2):
            cached_dots(s)
        for i, n in enumerate(SPREADS):
            if i == 0:
                pe.wait_ge(spread_ready, 1)
                pe.wait_ge(headrinv, 1)
            if i >= 2:
                pe.wait_ge(headread, i - 1)
            w = fused[0:HD, :] if n == "kid" else spread[:, n * P:(n + 1) * P]
            x = hT[0:HD, KI0] if n == "kid" else rstd[0:HROWS]
            for h in range(2):
                mm = nc.tensor.matmul(acc[:, (i % 2) * 2 + h, 0:H], w, x[:, h * H:(h + 1) * H], start=True, stop=True)
            mm.then_inc(headspread, 1)
            if i % 2 and 2 + i // 2 < S:
                cached_dots(2 + i // 2)
        pe.wait_ge(turned_copied, 7)
        pe.wait_ge(headread, 3)
        for s in range(S):
            half = (s % 2) * HD
            c = (s % 2) * 256 + (s // 2) * NIH
            mm = nc.tensor.matmul(acc[0:1, 6 + s % 2, c:c + NIH], kid[half:half + HD, T + s:T + s + 1],
                                  qis[half:half + HD, s, :], start=True, stop=True)
            if s == S - 2:
                mm.then_inc(kv_used, 2)
        mm.then_inc(sdots_done, 1)
        pe.wait_ge(headread, len(SPREADS))
        for j, m, w in QTILES[1:]:
            for i in range(NIH):
                v = (j - 1) * NIH + i
                half, slot = (i % 2) * HD, v % 2
                if v >= 2:
                    pe.wait_ge(relu_done, v - 1)
                parts = 2 if w > 512 else 1
                for b in range(parts):
                    mm = nc.tensor.matmul(acc[0:m, slot * 2 + b, 0:w // parts],
                                          hT[half:half + HD, QI0 + i // 2, j * P:j * P + m],
                                          kid[half:half + HD, b * (w // parts):(b + 1) * (w // parts)],
                                          start=True, stop=True)
                mm.then_inc(dots_done, 1)
        pe.wait_ge(sdots_read, 1)

        def count(n):
            pe.wait_ge(count_asked, n + 1)
            nc.tensor.matmul(acc[:, 6, 64:64 + S], ones_b[:], cnt_b[:], start=True, stop=True).then_inc(count_done, 1)

        def scores(s, quarter):
            if quarter == 0:
                if s >= 2:
                    pe.wait_ge(sscore_copied, s - 1)
                pe.wait_ge(sp_keys_loaded[s % 2], 16 * NPG // 2 * (s // 2 + 1))
                pe.wait_ge(pool_loaded[s % 2], 16 * NPG // 2 * (s // 2 + 1))
            for r in range(quarter * 4, quarter * 4 + 4):
                for t in range(2):
                    c = r * NH + t * 8
                    mm = nc.tensor.matmul(acc[:, 7 - 2 * (s % 2), c:c + 8], kv[:, s % 2, 2 * r + t::2 * NPG],
                                          qblk[:, s, t, :], start=True, stop=True)
            if quarter == 3:
                mm.then_inc(kv_used, 1)
                for t in range(2):
                    mm = nc.tensor.matmul(acc[0:1, 4, s * NH + t * 8:s * NH + t * 8 + 8], hT[:, K0 + t, T + s:T + s + 1],
                                          qblk[:, s, t, :], start=True, stop=True)
                mm.then_inc(sscore_done, 1)

        pe.wait_ge(turned_copied, 8)
        for n in range(32):
            count(n)
            scores(n // 4, n % 4)
        count(32)
        pe.wait_ge(count_asked, 34)
        nc.tensor.matmul(acc[:, 6, 128:128 + S], before_b[:], tie_b[:], start=True, stop=True)
        nc.tensor.matmul(acc[:, 6, 192:192 + S], ones_b[:], tie_b[:], start=True, stop=True).then_inc(count_done, 1)
        pe.wait_ge(sside, 1)
        nc.tensor.transpose(acc[:, 4, 0:P], smax[:], ident[:]).then_inc(sscore_done, 1)
        pe.wait_ge(sside, 2)
        nc.tensor.matmul(acc[:, 4, P:2 * P], ones[:], sdiag[:], start=True, stop=True).then_inc(sscore_done, 1)
        pe.wait_ge(sside, 3)
        nc.tensor.matmul(acc[:, 4, 2 * P:3 * P], ones[:], smax[:], start=True, stop=True).then_inc(sscore_done, 1)
        pe.wait_ge(sside, 4)

        units = [(j, m, w, pos) for j, m, w in QTILES for pos in range(NH)]

        def qk(u):
            j, m, w, pos = units[u]
            half, t = (pos % 2) * HD, pos // 2
            if u >= 2:
                pe.wait_ge(neg_ready, u - 1)
            parts = 2 if w > 512 else 1
            for b in range(parts):
                mm = nc.tensor.matmul(acc[0:m, (u % 2) * 2 + b, 0:w // parts],
                                      hT[half:half + HD, t, j * P:j * P + m],
                                      hT[half:half + HD, K0 + t // 4, b * (w // parts):(b + 1) * (w // parts)],
                                      start=True, stop=True)
            mm.then_inc(qk_done, 1)

        def turn(u):
            j, m, w, pos = units[u]
            pe.wait_ge(exp_done, u + 1)
            if u >= 2:
                pe.wait_ge(pt_ready[u % 2], u // 2)
            if pos < 2 and j >= 1:
                pe.wait_ge(ot_copied, j)
            for k in range(j + 1):
                kk = min(P, w - k * P)
                mm = nc.tensor.transpose(acc[0:kk, 4 + u % 2, k * m:(k + 1) * m], prob[0:m, u % 2, k * P:k * P + kk],
                                         ident[0:m, 0:m])
            mm.then_inc(pt_done, 1)

        def pv(u):
            j, m, w, pos = units[u]
            g = 2 * (pos // 8) + pos % 2
            pe.wait_ge(pt_ready[u % 2], u // 2 + 1)
            if pos == 0 and j >= 1:
                pe.wait_ge(orow_ready, j)
            for k in range(j + 1):
                kk = min(P, w - k * P)
                mm = nc.tensor.matmul(acc[0:m, 6 + pos // 8, (pos % 8) * HD:(pos % 8 + 1) * HD],
                                      probT[0:kk, u % 2, k * m:(k + 1) * m], vtok[0:kk, k, g * HD:(g + 1) * HD],
                                      start=(k == 0), stop=(k == j))
            mm.then_inc(pv_done, 1)

        def turn_output(j):
            m = QTILES[j][1]
            pe.wait_ge(orow_ready, j + 1)
            pe.wait_ge(pt_ready[0], 8 * (j + 1))
            pe.wait_ge(pt_ready[1], 8 * (j + 1))
            for t in range(QT):
                mm = nc.tensor.transpose(acc[:, 4 + t // 4, (t % 4) * P:(t % 4) * P + m], orow[0:m, t * P:(t + 1) * P],
                                         ident[0:m, 0:m])
            mm.then_inc(ot_done, 1)

        def sample_values(s):
            pe.wait_ge(pool_loaded[s % 2], 16 * (NPG // 2 * (S // 2) + s // 2 + 1))
            for r in range(NPG):
                for t in range(2):
                    mm = nc.tensor.matmul(acc[:, 1 + 2 * t, s * 8:(s + 1) * 8], kv[:, s % 2, r * 256 + t * P:r * 256 + (t + 1) * P],
                                          Ss[:, s, r, t * 8:(t + 1) * 8], start=(r == 0), stop=False)
            mm.then_inc(kv_used, 1)
            for t in range(2):
                mm = nc.tensor.matmul(acc[:, 1 + 2 * t, s * 8:(s + 1) * 8], vnew[0:1, s, t * P:(t + 1) * P],
                                      Ss[0:1, s, NPG, t * 8:(t + 1) * 8], start=False, stop=True)
            mm.then_inc(spv_done, 1)

        for j in range(5):
            lo, hi = NH * j, NH * (j + 1)
            pe.wait_ge(bias_ready, j + 1)
            if j == 4:
                pe.wait_ge(so_ready, 4)
            for u in range(lo, hi + 3):
                if u < hi:
                    qk(u)
                if lo <= u - 2 < hi:
                    turn(u - 2)
                if lo <= u - 3 < hi:
                    pv(u - 3)
                if 1 <= j < 4 and (u - lo) % 6 == 5 and (j - 1) * 3 + (u - lo) // 6 < S:
                    sample_values((j - 1) * 3 + (u - lo) // 6)
            turn_output(j)

    def act_attention(act):
        act.wait_ge(epilogue_done, BASE["attn_out"] + CREDIT)
        for n, t in enumerate(NORMED):
            if n >= 4:
                act.wait_ge(headsum, n - 3)
            nc.scalar.activation(scr[:, n % 4], hT[:, t], ACT.Square).then_inc(headsq, 1)
        act.wait_ge(headsum, len(NORMED))
        nc.scalar.activation(halves(rstd[0:HROWS]), acc[0:HROWS, 0:2, 0:H], ACT.Sqrt, bias=epsc[0:HROWS, 0:1],
                             scale=1.0 / HD).then_inc(headstd, 1)
        for j, m, w in QTILES[1:]:
            for i in range(NIH):
                v = (j - 1) * NIH + i
                act.wait_ge(dots_done, v + 1)
                if v >= 2:
                    act.wait_ge(wsum_done, v - 1)
                nc.scalar.activation(flat(j, neg_s[:, v % 2], m, w), wide(j, acc[:, (v % 2) * 2:(v % 2) * 2 + 2], m, w),
                                     ACT.Relu).then_inc(relu_done, 1)
        act.wait_ge(turned_copied, 6)
        for s in range(S):
            act.wait_ge(sscore_done, s + 1)
            nc.scalar.activation(Ss[:, s, 0:NPG, :], acc[:, 7 - 2 * (s % 2), 0:256].rearrange(
                "p (g h) -> p g h", g=NPG), ACT.Copy).then_inc(sscore_copied, 1)
        nc.scalar.activation(Ss[0:1, :, NPG, :], acc[0:1, 4, 0:S * NH].rearrange("p (s h) -> p s h", s=S),
                             ACT.Copy).then_inc(sscore_copied, 1)
        act.wait_ge(sexp_asked, S)
        nc.scalar.activation(Ss[:], Ss[:], ACT.Exp, scale=HD ** -0.5).then_inc(sexp_done, 1)
        units = [(j, m, w, pos) for j, m, w in QTILES for pos in range(NH)]

        def expo(u):
            j, m, w, pos = units[u]
            act.wait_ge(neg_ready, u + 1)
            if u >= 2:
                act.wait_ge(pt_done, u - 1)
            if pos == 0 and j:
                act.wait_ge(orow_ready, j)
            nc.scalar.activation(prob[0:m, u % 2, 0:w], neg_s[0:m, u % 2, 0:w], ACT.Exp, bias=rowmin[0:m, u % 2:u % 2 + 1],
                                 scale=-1.0, accum_out=rsum[0:m, pos:pos + 1]).then_inc(exp_done, 1)

        for j in range(5):
            lo, hi = NH * j, NH * (j + 1)
            for u in range(lo, hi + 1):
                if u < hi:
                    expo(u)
                if u - 1 >= lo and (u - 1) % 2 == 1:
                    copy_turned(act, nc.scalar.copy, u - 1, units)
            m = QTILES[j][1]
            act.wait_ge(ot_done, j + 1)
            nc.scalar.copy(hT[:, 0:QT, j * P:j * P + m], acc[:, 4:6, :].rearrange("p b (t c) -> p (b t) c", t=4)[:, :, 0:m]
                           ).then_inc(ot_copied, 1)
        act.wait_ge(so_ready, 4)
        act.wait_ge(ot_copied, 5)
        for t in range(QT):
            nc.scalar.activation(xh[:, t], hT[:, t], ACT.Copy).then_inc(at_xh, 1)

    def copy_turned(eng, copy, u, units):
        j, m, w, pos = units[u]
        eng.wait_ge(pt_done, u + 1)
        if u >= 2:
            eng.wait_ge(pv_done, u - 1)
        full = min(j + 1, 4)
        ins = copy(probT[:, u % 2, 0:full * m], acc[:, 4 + u % 2, 0:full * m])
        if j == 4:
            ins.then_inc(act_chain if eng is nc.scalar else dve_side, 1)
            ins = copy(probT[0:w - 4 * P, u % 2, 4 * m:5 * m], acc[0:w - 4 * P, 4 + u % 2, 4 * m:5 * m])
        ins.then_inc(pt_ready[u % 2], 1)

    def dve_attention(dve, chain):
        nc.vector.scalar_tensor_tensor(krow[:], pages[:], float(P), lane[:, 0:1].broadcast_to([P, S * NPG]),
                                       ALU.mult, ALU.add).then_inc(rows_ready, 1)
        nc.vector.scalar_tensor_tensor(vrow[:], vrow[:], 8.0, lane[:, 1:2].broadcast_to([P, S]),
                                       ALU.mult, ALU.add).then_inc(rows_ready, 1)
        nc.vector.tensor_copy(spread.rearrange("p (h d) -> p h d", d=HD),
                              ident[0:HROWS, 0:HROWS].unsqueeze(2).broadcast_to([HROWS, HROWS, HD])).then_inc(spread_ready, 1)
        dve.wait_ge(turned, 1)
        nc.vector.tensor_copy(vnew[0:1].rearrange("p s c -> p (s c)").rearrange("p (b c) -> p b c", b=4), acc[0:1, 0:4, :]
                              ).then_inc(turned_copied, 1)
        dve.wait_ge(turned, 2)
        nc.vector.tensor_copy(vtok[:, 0:4], acc[:, 4:6, :].rearrange("p b (j c) -> p (b j) c", j=2)).then_inc(turned_copied, 1)
        nc.vector.tensor_copy(vtok[0:24, 4], acc[0:24, 6, 0:256]).then_inc(turned_copied, 1)
        wscale = (HD ** -0.5) * (NIH ** -0.5)
        nc.vector.tensor_scalar(wtok[:, 0:4], acc[:, 7, 0:32].rearrange("p (j h) -> p j h", h=NIH), wscale, None, ALU.mult
                                ).then_inc(dve_side, 1)
        chain.link(nc.vector.tensor_scalar(wtok[0:24, 4], acc[0:24, 7, 32:40], wscale, None, ALU.mult))
        nc.vector.tensor_tensor(wsel[:], wtok[0:24, 4].unsqueeze(1).broadcast_to([24, S, NIH]),
                                ident[0:24, 16:24].unsqueeze(2).broadcast_to([24, S, NIH]), ALU.mult).then_inc(turned_copied, 1)
        for half in range(2):
            rows = slice(half * HD, half * HD + HD)
            own = hT[rows, QI0:QI0 + QIT, T:N].rearrange("p i s -> p s i")
            other = acc[rows, 7, 64:96].rearrange("p (i s) -> p s i", s=S)
            view = qis[rows].rearrange("p s (i e) -> p s i e", e=2)
            nc.vector.tensor_copy(view[:, :, :, half], own).then_inc(dve_side, 1)
            ins = nc.vector.tensor_copy(view[:, :, :, 1 - half], other)
            ins.then_inc(turned_copied if half else dve_side, 1)
        nc.vector.memset(Ss[:, :, NPG, :], -BIG).then_inc(turned_copied, 1)
        nc.vector.memset(scs[:, :, NPG], -BIG).then_inc(dve_side, 1)
        nc.vector.memset(qblk[:], 0.0).then_inc(dve_side, 1)
        dve.wait_ge(turned, 3)
        nc.vector.tensor_copy(wib[:].rearrange("p s h -> p (s h)"), acc[:, 7, 128:192]).then_inc(turned_copied, 1)
        dve.wait_ge(headstd, 1)
        nc.vector.reciprocal(rstd[0:HROWS], rstd[0:HROWS]).then_inc(headrinv, 1)
        for i, n in enumerate(SPREADS):
            dve.wait_ge(headspread, i + 1)
            a = acc[:, (i % 2) * 2:(i % 2) * 2 + 2, 0:H]
            if n == "kid":
                nc.vector.tensor_copy(halves(kid[:]), a).then_inc(headread, 1)
                continue
            t = NORMED[n]
            rows = HD if t == KI0 else P
            gain = headg[0:rows, 2:3] if t == KI0 else headg[0:rows, 1:2] if t >= K0 else headg[0:rows, 0:1]
            x = halves(hT[0:rows, t])
            nc.vector.scalar_tensor_tensor(x, x, gain, a[0:rows], ALU.mult, ALU.mult).then_inc(headread, 1)
        dve.wait_ge(headread, len(SPREADS))
        for t in range(2):
            for half in range(2):
                rows = slice(half * HD, half * HD + HD)
                ins = nc.vector.tensor_copy(qblk[rows, :, t, 4 * half:4 * half + 4],
                                            hT[rows, 4 * t:4 * t + 4, T:N].rearrange("p r s -> p s r"))
                ins.then_inc(turned_copied if t and half else dve_side, 1)
        for j, m, w in QTILES[1:]:
            for i in range(NIH):
                v = (j - 1) * NIH + i
                dve.wait_ge(relu_done, v + 1)
                row, wt = bias[0:m, j - 1, 0:w], wtok[0:m, j, i:i + 1]
                if i == 0:
                    ins = nc.vector.tensor_scalar(row, neg_s[0:m, v % 2, 0:w], wt, None, ALU.mult)
                else:
                    dve.wait_ge(wsum_done, v)
                    ins = nc.vector.scalar_tensor_tensor(row, neg_s[0:m, v % 2, 0:w], wt, row, ALU.mult, ALU.add)
                ins.then_inc(wsum_done, 1)
            dve.wait_ge(wsum_done, j * NIH)
            diag = bias[0:m, j - 1, j * P:j * P + m]
            chain.link(nc.vector.tensor_tensor(diag, diag, negm[0:m, 0:m], ALU.add))
        prod = scr[:, 0:2].rearrange("p a n -> p (a n)")[:, 0:S * P].rearrange("p (s g h) -> p s g h", s=S, g=NPG)
        for s in range(S):
            dve.wait_ge(sdots_done, S + 1)
            dots = acc[:, 4 + s % 2, (s // 2) * P:(s // 2 + 1) * P].rearrange("p (g h) -> p g h", g=NPG)
            ins = nc.vector.scalar_tensor_tensor(prod[:, s], dots, 0.0,
                                                 wib[:, s].unsqueeze(1).broadcast_to([P, NPG, NIH]), ALU.max, ALU.mult)
            if s < S - 1:
                ins.then_inc(dve_side, 1)
        chain.link(ins)
        nc.vector.tensor_reduce(scs[:, :, 0:NPG], prod, AX.X, ALU.add).then_inc(dve_side, 1)
        own = scr[0:1, 2, 0:S * NIH]
        for e in range(2):
            dots = acc[0:1, 6 + e, e * 256:e * 256 + 32].rearrange("p (s h) -> p s h", h=NIH)
            chain.link(nc.vector.scalar_tensor_tensor(
                own.rearrange("p (s e h) -> p s e h", e=2, h=NIH)[:, :, e], dots, 0.0,
                wib[0:1].rearrange("p (s e) h -> p s e h", e=2)[:, :, e], ALU.max, ALU.mult))
        chain.link(nc.vector.tensor_reduce(scs[0:1, :, NPG], own.rearrange("p (s h) -> p s h", s=S), AX.X, ALU.add))
        chain.link(nc.vector.tensor_scalar(scs[:], scs[:], 0.0, None, ALU.add))
        bits = scs[:].bitcast(I32)
        chain.link(nc.vector.tensor_scalar(kmask[:], bits, 31, -2 ** 31, ALU.arith_shift_right, ALU.bitwise_or))
        chain.link(nc.vector.tensor_tensor(keys[:], bits, kmask[:], ALU.bitwise_xor))
        ukeys, umask = keys[:].bitcast(U32), kmask[:].bitcast(U32)
        chain.link(nc.vector.tensor_scalar(umask, ukeys, 16, None, ALU.logical_shift_right))
        chain.link(nc.vector.tensor_copy(khi[:], umask))
        chain.link(nc.vector.tensor_scalar(umask, ukeys, 0xFFFF, None, ALU.bitwise_and))
        nc.vector.tensor_copy(klo[:], umask).then_inc(sdots_read, 1)
        dve.wait_ge(sdots_read, 1)
        chain.link(nc.vector.memset(cand[:], 2.0 ** 15))
        hit = prod.rearrange("p s g h -> p (s g h)")[:, 0:S * SKEYS].rearrange("p (s g) -> p s g", s=S)

        def over_groups(ap):
            return ap.unsqueeze(2).broadcast_to([P, S, SKEYS])

        taken = chosen = None
        for j, m, w in QTILES[1:]:
            row = bias[0:m, j - 1, 0:w]

            def largest():
                if taken:
                    chain.after(taken)
                return chain.mark(nc.vector.max(top8[0:m], row))

            def take_away(found):
                chain.after(found)
                return chain.mark(nc.vector.match_replace(row, top8[0:m], row, GONE))

            for r in range(0, TOPK_P // 8, 2):
                n = ((j - 1) * (TOPK_P // 8) + r) // 2
                b = 15 - n % 16
                found = largest()
                if chosen:
                    chain.after(chosen)
                hits = chain.mark(nc.vector.tensor_tensor(hit, khi[:], over_groups(cand[:]), ALU.is_ge))
                taken = take_away(found)
                chain.after(hits)
                with nc.allow_low_precision(reason="counts up to 17 are exact in bfloat16"):
                    nc.vector.tensor_reduce(cnt_b[:], hit, AX.X, ALU.add).then_inc(count_asked, 1)
                found = largest()
                dve.wait_ge(count_done, n + 1)
                stepped = chain.mark(nc.vector.tensor_scalar(step[:], acc[:, 6, 64:64 + S], TOPK_S - 0.5, 2.0 ** b,
                                                             ALU.is_ge, ALU.mult))
                taken = take_away(found)
                chain.after(stepped)
                chosen = chain.mark(nc.vector.scalar_tensor_tensor(
                    cand[:], step[:], -(2.0 ** (b - 1)) if b else -1.0, cand[:], ALU.add, ALU.add))
                if n == 15:
                    chain.after(chosen)
                    chain.link(nc.vector.tensor_tensor(hit, khi[:], over_groups(cand[:]), ALU.subtract))
                    chain.link(nc.vector.tensor_scalar(hit, hit, -1.0, 1.0, ALU.max, ALU.min))
                    nc.vector.scalar_tensor_tensor(khi[:], hit, 65536.0, klo[:], ALU.mult, ALU.add).then_inc(dve_side, 1)
                    chosen = chain.mark(nc.vector.memset(cand[:], 2.0 ** 15))
            chain.after(taken)
            nc.vector.tensor_scalar(row, row, GONE / 1.5, -BIG, ALU.is_gt, ALU.mult).then_inc(dve_side, 1)
            taken = None
        chain.after(chosen)
        gt = klo
        chain.link(nc.vector.tensor_tensor(gt[:], khi[:], over_groups(cand[:]), ALU.is_gt))
        with nc.allow_low_precision(reason="counts up to 17 are exact in bfloat16"):
            nc.vector.tensor_reduce(cnt_b[:], gt[:], AX.X, ALU.add).then_inc(count_asked, 1)
        chain.link(nc.vector.tensor_tensor(rank[:], khi[:], over_groups(cand[:]), ALU.is_equal))
        with nc.allow_low_precision(reason="counts up to 16 are exact in bfloat16"):
            nc.vector.tensor_reduce(tie_b[:], rank[:, :, 0:NPG], AX.X, ALU.add).then_inc(count_asked, 1)
        chain.link(nc.vector.memset(khi[:, :, 0], 0.0))
        for g in range(NPG):
            chain.link(nc.vector.tensor_tensor(khi[:, :, g + 1], khi[:, :, g], rank[:, :, g], ALU.add))
        dve.wait_ge(count_done, 34)
        chain.link(nc.vector.tensor_scalar(step[:], acc[:, 6, 64:64 + S], -1.0, float(TOPK_S), ALU.mult, ALU.add))
        chain.link(nc.vector.tensor_tensor(khi[:, :, 0:NPG], khi[:, :, 0:NPG], acc[:, 6, 128:128 + S].unsqueeze(2).broadcast_to(
            [P, S, NPG]), ALU.add))
        chain.link(nc.vector.tensor_scalar(khi[:, :, NPG], acc[:, 6, 192:192 + S], 1.0, None, ALU.mult))
        chain.link(nc.vector.tensor_tensor(khi[:], khi[:], over_groups(step[:]), ALU.is_lt))
        chain.link(nc.vector.tensor_tensor(khi[:], khi[:], rank[:], ALU.mult))
        chain.link(nc.vector.tensor_tensor(khi[:], khi[:], gt[:], ALU.add))
        chain.link(nc.vector.tensor_scalar(khi[:], khi[:], 1.0, BIG, ALU.subtract, ALU.mult))
        dve.wait_ge(sscore_copied, S + 1)
        chain.link(nc.vector.tensor_tensor(Ss[:], Ss[:], khi[:].unsqueeze(3).broadcast_to([P, S, SKEYS, NH]), ALU.add))
        smax3 = smax[:].rearrange("p (s h) -> p s h", s=S)
        nc.vector.tensor_reduce(smax3, Ss[:].rearrange("p s g h -> p s h g"), AX.X, ALU.max).then_inc(sside, 1)
        dve.wait_ge(sscore_done, S + 1)
        chain.link(nc.vector.tensor_reduce(srow[:], acc[:, 4, 0:P], AX.X, ALU.max))
        nc.vector.tensor_scalar(sdiag[:], ident[:], srow[:, 0:1], None, ALU.mult).then_inc(sside, 1)
        dve.wait_ge(sscore_done, S + 2)
        top = acc[:, 4, P:2 * P].rearrange("p (s h) -> p s h", s=S)
        for s in range(S):
            ins = nc.vector.tensor_tensor(Ss[:, s], Ss[:, s], top[:, s].unsqueeze(1).broadcast_to([P, SKEYS, NH]), ALU.subtract)
            ins.then_inc(sexp_asked, 1)
        nc.vector.memset(credit[:, 3:4], 0.0).then_inc(bias_ready, 5)
        dve.wait_ge(sexp_done, 1)
        nc.vector.tensor_reduce(smax3, Ss[:].rearrange("p s g h -> p s h g"), AX.X, ALU.add).then_inc(sside, 1)
        dve.wait_ge(sscore_done, S + 3)
        nc.vector.reciprocal(srinv[:].rearrange("p s h -> p (s h)"), acc[:, 4, 2 * P:3 * P]).then_inc(sside, 1)

        units = [(j, m, w, pos) for j, m, w in QTILES for pos in range(NH)]

        def masked(u):
            j, m, w, pos = units[u]
            dve.wait_ge(qk_done, u + 1)
            if u >= 2:
                dve.wait_ge(exp_done, u - 1)
            b = negm[0:m, 0:w] if j == 0 else bias[0:m, j - 1, 0:w]
            nc.vector.tensor_tensor_reduce(flat(j, neg_s[:, u % 2], m, w), wide(j, acc[:, (u % 2) * 2:(u % 2) * 2 + 2], m, w),
                                           b.rearrange("p (a n) -> p a n", a=2 if w > 512 else 1),
                                           -(HD ** -0.5), -GONE, ALU.add, ALU.min,
                                           accum_out=rowmin[0:m, u % 2:u % 2 + 1]).then_inc(neg_ready, 1)

        for j in range(5):
            lo, hi = NH * j, NH * (j + 1)
            m = QTILES[j][1]
            for u in range(lo, hi + 2):
                if u < hi:
                    masked(u)
                if lo <= u - 2 < hi and u % 2 == 0:
                    copy_turned(dve, nc.vector.tensor_copy, u - 2, units)
            if j == 3:
                dve.wait_ge(spv_done, S)
                for t in range(2):
                    for half in range(2):
                        rows = slice(half * HD, half * HD + HD)
                        o = acc[rows, 1 + 2 * t, 0:S * 8].rearrange("p (s c) -> p c s", s=S)[:, 4 * half:4 * half + 4, :]
                        r = srinv[rows].rearrange("p s c -> p c s")[:, t * 8 + 4 * half:t * 8 + 4 * half + 4, :]
                        nc.vector.tensor_tensor(hT[rows, 4 * t:4 * t + 4, T:N], o, r, ALU.mult).then_inc(so_ready, 1)
            dve.wait_ge(pv_done, hi)
            chain.link(nc.vector.reciprocal(rinv[0:m], rsum[0:m]))
            if j:
                dve.wait_ge(ot_done, j)
            nc.vector.tensor_tensor(orow[0:m].rearrange("p (h d) -> p h d", h=NH),
                                    acc[0:m, 6:8, :].rearrange("p b (h d) -> p (b h) d", d=HD),
                                    rinv[0:m].unsqueeze(2).broadcast_to([m, NH, HD]), ALU.mult).then_inc(orow_ready, 1)

    def pool_attention(pool):
        pool_keys_values(pool)
        for t in range(QT):
            pool.wait_ge(at_xh, t + 1)
            nc.gpsimd.tensor_tensor(xl[:, t], hT[:, t], xh[:, t].bitcast(F32), ALU.subtract).then_inc(at_xl, 1)

    def pool_consts(pool, chain):
        nc.gpsimd.memset(credit[:, 0:1], 0.0).then_inc(chunk_done, CREDIT)
        chain.link(nc.gpsimd.memset(ident[:], 0.0))
        chain.link(nc.gpsimd.affine_select(ident[:], ident[:], [[-1, P]], ALU.not_equal, 1.0, base=0, channel_multiplier=1))
        chain.link(nc.gpsimd.memset(negm[:], 0.0))
        chain.link(nc.gpsimd.affine_select(negm[:], negm[:], [[-1, P]], ALU.is_ge, -BIG, base=0, channel_multiplier=1))
        chain.link(nc.gpsimd.memset(pick[:], 0.0))
        for half in range(2):
            chain.link(nc.gpsimd.memset(pick[half * HD:half * HD + HD, PICK + half:PICK + half + 1], 1.0))
        for a in range(2):
            r = slice(a * HD, a * HD + HD)
            chain.link(nc.gpsimd.tensor_copy(swap[:, r], ident[:, HD - a * HD:P - a * HD]))
            chain.link(nc.gpsimd.tensor_copy(fused[:, r], ident[:, 0:HD]))
        chain.link(nc.gpsimd.memset(ones_b[:], 1.0))
        chain.link(nc.gpsimd.memset(before_b[:], 1.0))
        chain.link(nc.gpsimd.affine_select(before_b[:], before_b[:], [[1, P]], ALU.is_gt, 0.0, base=0, channel_multiplier=-1))
        chain.link(nc.gpsimd.memset(upto1[:], 1.0))
        nc.gpsimd.affine_select(upto1[:], upto1[:], [[1, P]], ALU.is_ge, 0.0, base=0, channel_multiplier=-1).then_inc(consts, 1)

    kv_out_done = sem("kv_out_done")

    def sp_attention_outputs(sp):
        sp.wait_ge(headread, len(SPREADS))
        for name, t, n in (("kT", K0, KT2), ("vT", V0, VT2)):
            sp.dma_start(O[name].rearrange("(t p) n -> p t n", p=P), hT[:, t:t + n]).then_inc(kv_out_done, 16)
        sp.dma_start(O["kiT"], hT[0:HD, KI0]).then_inc(kv_out_done, 16)

    conv_ready, conv_used = sem("conv_ready"), sem("conv_used")
    params_loaded, dt_turned, dt_ready = sem("params_loaded"), sem("dt_turned"), sem("dt_ready")
    dt_e, dt_x = sem("dt_e"), sem("dt_x")
    cum_done, cum_read, decay_ready = sem("cum_done"), sem("cum_read"), sem("decay_ready")
    xturned, xr_ready, xd_ready = sem("xturned"), sem("xr_ready"), sem("xd_ready")
    cb_done, cb_ready = sem("cb_done"), sem("cb_ready")
    ab_done, ec_ready, cs_ready = sem("ab_done"), sem("ec_ready"), sem("cs_ready")
    arg_ready, e_ready, m_ready = sem("arg_ready"), sem("e_ready"), sem("m_ready")
    y_done, st_done, y_read, h_ready = sem("y_done"), sem("st_done"), sem("y_read"), sem("h_ready")
    ssd_out_done, sx_done, sx_ready = sem("ssd_out_done"), sem("sx_done"), sem("sx_ready")
    hs_loaded = [sem("hs_loaded0"), sem("hs_loaded1")]
    bc_done, bx_ready, hs_decayed, hs_ready = sem("bc_done"), sem("bx_ready"), sem("hs_decayed"), sem("hs_ready")
    hc_ready = sem("hc_ready")
    hs_stored = [sem("hs_stored0"), sem("hs_stored1")]
    gated, gsq, gsum_ready, gsum_done, gstd = sem("gated"), sem("gsq"), sem("gsum_ready"), sem("gsum_done"), sem("gstd")
    yn_ready, yh_ready, yl_ready = sem("yn_ready"), sem("yh_ready"), sem("yl_ready")
    SSD_STORES = 3
    CONVS = 2 * 12
    BX, BC = XT, XT + BT
    scrf = scr[:].rearrange("p a n -> p (a n)")
    half_scr = scrf.rearrange("p (u n) -> p u n", u=2)
    stage, conv = half_scr[:, :, 0:3 + N], half_scr[:, :, 3 + N:3 + N + T]
    Btok, CBm = scrf[:, 0:512], scrf[:, 512:768].rearrange("p (a l) -> p a l", a=2)
    dtx, dax = (scrf[:, 768 + 128 * a:896 + 128 * a].rearrange("p (t s) -> p t s", s=S) for a in range(2))
    ysam = scrf[:, 1024:1152].rearrange("p (t s) -> p t s", s=S)
    SCHUNKS = [(c, min(P, T - c * P)) for c in range(5)]
    GAIN, GEXP = XT // SG, SH // SG

    def sp_ssd(sp):
        k = NORM["ssd"]
        def params():
            sp.wait_ge(epilogue_done, BASE["ssd_in"] + CREDIT)
            for dst, name in ((convw, "conv_w"), (convb, "conv_b"), (window, "state_conv"), (featp, "feature_params")):
                sp.dma_start(dst[:].rearrange({2: "p a -> p a", 3: "p a b -> p (a b)", 4: "p a b c -> p (a b c)"}[len(dst.shape)]),
                             I[name]).then_inc(params_loaded, 16)
            sp.dma_start(headp[:].rearrange("p a b -> p (a b)"), I["head_params"].partition_broadcast(P).rearrange(
                "p a b -> p (a b)")).then_inc(params_loaded, 16)

        sp_stream(sp, "ssd_in", I["w_ssd_in"], BLK * P, between=params)
        base = BASE["ssd_out"]
        for u in range(2):
            sp.wait_ge(wl_ready, base + u - 1)
            sp.dma_start(raw[:, (base + u) % 2], I["w_ssd_out"][u]).then_inc(w_loaded[(base + u) % 2], 16)
        sp.wait_ge(conv_used, CREDIT + CONVS + 1)
        sp.dma_start(O["conv_prompt"], tail[:].rearrange("p a b -> p (a b)")).then_inc(ssd_out_done, 16)
        sp.dma_start(O["conv_sample"], window[:].rearrange("p a b c -> p (a b c)")).then_inc(ssd_out_done, 16)
        sp.wait_ge(h_ready, SG * 5)
        sp.dma_start(O["hT"], hst[:].rearrange("p h d -> p (h d)")).then_inc(ssd_out_done, 16)
        sp.wait_ge(y_read, SG * 5)
        sp.wait_ge(ssd_out_done, 48)
        for s in range(S):
            if s >= 2:
                sp.wait_ge(hc_ready, s - 1)
                sp.wait_ge(hs_stored[s % 2], 16 * (s // 2))
            sp.dma_start(hs[:, s % 2], I["state_ssm"][s]).then_inc(hs_loaded[s % 2], 16)
            if s >= 1:
                store_state(sp, s - 1)
        store_state(sp, S - 1)
        for e in range(2):
            sp.wait_ge(hs_stored[e], 16 * S // 2)
        for u in range(2, COUNT["ssd_out"]):
            sp.wait_ge(wl_ready, base + u - 1)
            sp.dma_start(raw[:, (base + u) % 2], I["w_ssd_out"][u]).then_inc(w_loaded[(base + u) % 2], 16)

    def store_state(sp, s):
        sp.wait_ge(hs_ready, s + 1)
        sp.dma_start(O["hs"][s], hs[:, s % 2]).then_inc(hs_stored[s % 2], 16)

    def pe_ssd(pe):
        k = NORM["ssd"]

        def normed(kt):
            pe.wait_ge(xl_ready, DT * k + kt + 1)

        pe_pairs(pe, "ssd_in", normed, 0, 12)
        pe_pairs(pe, "ssd_in", normed, 12, 1, 1)
        pe_pairs(pe, "ssd_in", normed, 13, 8)
        pe.wait_ge(epilogue_done, BASE["ssd_out"] + CREDIT)
        for c, m in SCHUNKS:
            m = m + S if c == 4 else m
            mm = nc.tensor.transpose(acc[0:m, 7, c * SH:(c + 1) * SH], sq[0:SH, c * P:c * P + m], ident[0:SH, 0:SH])
        mm.then_inc(dt_turned, 1)
        pe.wait_ge(dt_ready, 1)
        pe.wait_ge(conv_used, CREDIT + CONVS + 1)
        for c, m in SCHUNKS:
            cols = slice(c * P, c * P + m)
            if c:
                pe.wait_ge(y_read, SG * c)
                pe.wait_ge(h_ready, SG * c)
            nc.tensor.matmul(acc[0:m, 5, 0:SH], upto1[0:m, 0:m], dA[0:m, c, :], start=True, stop=True)
            nc.tensor.matmul(acc[:, 5, SH:2 * SH], ones[0:m, :], dA[0:m, c, :], start=True, stop=True).then_inc(cum_done, 1)
            for t in range(XT + BT):
                mm = nc.tensor.transpose(acc[0:m, t // 4, (t % 4) * P:(t % 4 + 1) * P], xbc[:, t, cols], ident[:])
            mm.then_inc(xturned, 1)

            def ab(b):
                pe.wait_ge(arg_ready, 8 * c + b - 1) if 8 * c + b >= 2 else None
                for i in range(4):
                    h = 4 * b + i
                    mm = nc.tensor.matmul(acc[:, 6 + b % 2, i * m:(i + 1) * m], dA[0:m, c, h:h + 1].broadcast_to([m, P]),
                                          upto1[0:m, 0:m], start=True, stop=True)
                mm.then_inc(ab_done, 1)

            def cb(g):
                nc.tensor.matmul(acc[0:m, 4 + g % 2, 0:m], xbc[:, BX + g, cols], xbc[:, BC + g, cols],
                                 start=True, stop=True).then_inc(cb_done, 1)

            def y(b):
                g = b // 2
                pe.wait_ge(m_ready, 8 * c + b + 1)
                if c:
                    pe.wait_ge(cs_ready, 8 * (c - 1) + b + 1)
                if b % 2 == 0 and g >= 2:
                    pe.wait_ge(y_read, SG * c + g - 1)
                for i in range(4):
                    h = 4 * b + i
                    rows = slice((h % 2) * HD, (h % 2) * HD + HD)
                    out = acc[rows, g % 2, (h // 2 % 4) * P:(h // 2 % 4) * P + m]
                    mm = nc.tensor.matmul(out, xr[0:m, h, :], Et[0:m, b % 2, i, 0:m], start=True, stop=(c == 0))
                    if c:
                        mm = nc.tensor.matmul(out, hst[:, h, :], Ct[:, b % 2, i, 0:m], start=False, stop=True)
                mm.then_inc(y_done, 1)

            def state(g):
                pe.wait_ge(xd_ready, c + 1)
                if g >= 2:
                    pe.wait_ge(h_ready, SG * c + g - 1)
                nc.tensor.matmul(acc[:, 2 + g % 2, :], Btok[0:m, g * P:(g + 1) * P],
                                 xd[0:m, g * GEXP:(g + 1) * GEXP, :].rearrange("p h d -> p (h d)"),
                                 start=True, stop=True).then_inc(st_done, 1)

            pe.wait_ge(cum_read, c + 1)
            pe.wait_ge(xr_ready, 2 * (c + 1))
            for b in range(9):
                if b < 8:
                    if b % 2 == 0:
                        if b >= 4:
                            pe.wait_ge(cb_ready, SG * c + b // 2 - 1)
                        cb(b // 2)
                    ab(b)
                if b >= 1:
                    y(b - 1)
                    if b % 2 == 0:
                        state(b // 2 - 1)
        pe.wait_ge(y_read, SG * 5)
        pe.wait_ge(h_ready, SG * 5)
        pe.wait_ge(sx_ready, 1)
        for h in range(SH):
            rows = slice((h % 2) * HD, (h % 2) * HD + HD)
            for a, src in enumerate((dtok[0:24, 4, h:h + 1], decay[0:24, h:h + 1])):
                mm = nc.tensor.matmul(acc[rows, a, h // 2 * S:(h // 2 + 1) * S], src.broadcast_to([24, HD]),
                                      ident[0:24, 16:24], start=True, stop=True)
        mm.then_inc(sx_done, 1)
        for s in range(S):
            if s >= 2:
                pe.wait_ge(hc_ready, s - 1)
            for a, first in enumerate((BX, BC)):
                for g in range(SG):
                    mm = nc.tensor.matmul(acc[:, 2 + 2 * a + s % 2, g * P:(g + 1) * P],
                                          xbc[:, first + g, T + s:T + s + 1].broadcast_to([P, P]), ident[:],
                                          start=True, stop=True)
            mm.then_inc(bc_done, 1)
        for g in range(SG):
            pe.wait_ge(gsum_ready, g + 1)
            if g == 0:
                pe.wait_ge(hc_ready, S)
            if g >= 2:
                pe.wait_ge(gstd, g - 1)
            for h in range(2):
                mm = nc.tensor.matmul(acc[:, (g % 2) * 2 + h, 0:H], ones[:], ssum[:, h * H:(h + 1) * H], start=True, stop=True)
            mm.then_inc(gsum_done, 1)
        pe.wait_ge(gstd, SG)
        pe_singles(pe, "ssd_out", XT, lambda kt: yh[:, kt], lambda kt: yl[:, kt], lambda kt: pe.wait_ge(yl_ready, kt + 1))

    def act_ssd(act):
        base = BASE["ssd_in"]
        act.wait_ge(params_loaded, 16 * 5)

        def conv_chunk(i, u):
            n, slot = base + u, (base + u) % 2
            act_round(act, base + 1, i, u)
            act.wait_ge(conv_ready, i * 2 + (2 * u + 2))
            act.wait_ge(chunk_done, i + (n + 1 + CREDIT))
            nc.scalar.activation(stage[:, :, 3:3 + N].rearrange("p t (h n) -> p t h n", h=2),
                                 acc[:, slot * 4:slot * 4 + 4, 0:H].rearrange("p (t h) n -> p t h n", h=2),
                                 ACT.Copy).then_inc(epilogue_done, 1)
            for t in range(2):
                act.wait_ge(conv_ready, i * 2 + (2 * u + 3 + t))
                act.wait_ge(params_loaded, 16)
                nc.scalar.activation(xbc[:, ds(i * 2 + (2 * u + t), 1), 0:T].rearrange("p a n -> p (a n)"),
                                     conv[:, t], ACT.Silu, bias=convb[:, ds(i * 2 + (2 * u + t), 1)]).then_inc(conv_used, 1)

        chunks(act, 12, conv_chunk)
        act.wait_ge(conv_ready, CREDIT + CONVS + 1)
        nc.scalar.activation(xbc[:, :, T:N], sconv, ACT.Silu).then_inc(conv_used, 1)
        act_round(act, base + 13, 0, 0)

        def gate_chunk(i, u):
            n, slot = base + 13 + u, (base + 13 + u) % 2
            act_round(act, base + 14, i, u)
            act.wait_ge(chunk_done, i + (n + 1 + CREDIT))
            act.wait_ge(params_loaded, 16)
            nc.scalar.activation(zT[:, ds(i * 2 + 2 * u, 2)].rearrange("p t (h n) -> p (t h) n", h=2),
                                 acc[:, slot * 4:slot * 4 + 4, 0:H], ACT.Silu).then_inc(epilogue_done, 1)

        chunks(act, 8, gate_chunk)
        e, u1 = dtmp[:, 1], dtmp[:, 2]
        act.wait_ge(dt_x, 1)
        nc.scalar.activation(e, dtmp[:, 0], ACT.Exp, scale=-1.0).then_inc(dt_e, 1)
        act.wait_ge(dt_x, 2)
        nc.scalar.activation(dtmp[:, 3], u1, ACT.Ln).then_inc(dt_e, 1)
        nc.scalar.activation(headp[:, 1], headp[:, 1], ACT.Exp).then_inc(dt_e, 1)
        for c, m in SCHUNKS:
            act.wait_ge(cum_read, c + 1)
            nc.scalar.activation(cdecay[:], cum[:, 1], ACT.Exp).then_inc(decay_ready, 1)
            nc.scalar.activation(decay[0:m], decay[0:m], ACT.Exp).then_inc(decay_ready, 1)
            for b in range(8):
                k = 8 * c + b
                act.wait_ge(ab_done, k + 1)
                if c and k - 8 >= 2:
                    act.wait_ge(y_done, k - 1)
                src = acc[:, 6 + b % 2, 0:4 * m].rearrange("p (i l) -> p i l", i=4)
                if c:
                    nc.scalar.activation(Ct[:, b % 2, :, 0:m], src, ACT.Exp).then_inc(ec_ready, 1)
                act.wait_ge(arg_ready, k + 1)
                nc.scalar.activation(Et[0:m, b % 2, :, 0:m], Et[0:m, b % 2, :, 0:m], ACT.Exp).then_inc(e_ready, 1)
        act.wait_ge(h_ready, SG * 5)
        nc.scalar.activation(decay[0:24], dA[0:24, 4], ACT.Exp).then_inc(sx_ready, 1)
        for g in range(SG):
            for t in range(GAIN):
                n = g * GAIN + t
                act.wait_ge(gated, n + 1)
                if n >= 1:
                    act.wait_ge(gsum_step, n)
                nc.scalar.activation(sq[:], xbc[:, n], ACT.Square).then_inc(gsq, 1)
            act.wait_ge(gsum_done, g + 1)
            if g:
                act.wait_ge(yn_ready, GAIN * g)
            nc.scalar.activation(halves(rstd[:]), acc[:, (g % 2) * 2:(g % 2) * 2 + 2, 0:H], ACT.Sqrt, bias=epsc[:, 0:1],
                                 scale=SG / DI).then_inc(gstd, 1)
            for t in range(GAIN):
                n = g * GAIN + t
                act.wait_ge(yn_ready, n + 1)
                if n == 0:
                    for e in range(2):
                        act.wait_ge(hs_stored[e], 16 * S // 2)
                nc.scalar.activation(yh[:, n], xbc[:, n], ACT.Copy).then_inc(yh_ready, 1)
        act_rounds(act, "ssd_out")

    def dve_ssd(dve, chain):
        base = BASE["ssd_in"]
        k = NORM["ssd"]
        dve.wait_ge(params_loaded, 16 * 5)
        dve.wait_ge(xl_ready, DT * k + DT)
        nc.vector.memset(stage[:, :, 0:3], 0.0).then_inc(conv_ready, CREDIT)
        nc.vector.memset(credit[:, 3:4], 0.0).then_inc(conv_used, CREDIT)
        dve.wait_ge(conv_ready, 2)

        def conv_chunk(i, u):
            n, slot = base + u, (base + u) % 2
            dve_rest(dve, base + 1, i, u)
            dve.wait_ge(epilogue_done, i + (n + 1 + CREDIT))
            for t in range(2):
                def w(j):
                    return convw[:, ds(i * 2 + (2 * u + t), 1), j]
                dve.wait_ge(conv_used, i * 2 + (2 * u + t + 1))
                chain.link(nc.vector.tensor_scalar(conv[:, t], stage[:, t, 0:T], w(0), None, ALU.mult))
                chain.link(nc.vector.scalar_tensor_tensor(conv[:, t], stage[:, t, 1:1 + T], w(1), conv[:, t], ALU.mult, ALU.add))
                chain.link(nc.vector.scalar_tensor_tensor(conv[:, t], stage[:, t, 2:2 + T], w(2), conv[:, t], ALU.mult, ALU.add))
                tile = ds(i * 2 + (2 * u + t), 1)
                nc.vector.tensor_scalar(window[:, tile, :, 3].rearrange("p a s -> p (a s)"), stage[:, t, 3 + T:3 + N], 1.0, None,
                                        ALU.mult).then_inc(dve_side, 1)
                nc.vector.tensor_scalar(tail[:, tile, :].rearrange("p a s -> p (a s)"), stage[:, t, T:T + 3], 1.0, None,
                                        ALU.mult).then_inc(dve_side, 1)
                nc.vector.scalar_tensor_tensor(conv[:, t], stage[:, t, 3:3 + T], w(3), conv[:, t], ALU.mult, ALU.add
                                               ).then_inc(conv_ready, 1)

        chunks(dve, 12, conv_chunk, chain, 6)
        dve.wait_ge(conv_used, CREDIT + CONVS)
        dve.wait_ge(conv_ready, CREDIT + CONVS)
        chain.link(nc.vector.tensor_tensor(swork, window[:], convw[:].unsqueeze(2).broadcast_to([P, CVT, S, 4]), ALU.mult))
        chain.link(nc.vector.tensor_reduce(sconv, swork, AX.X, ALU.add))
        nc.vector.tensor_tensor(sconv, sconv, convb[:].unsqueeze(2).broadcast_to([P, CVT, S]), ALU.add).then_inc(conv_ready, 1)
        n = base + 12
        dve_rest(dve, base + 13, 0, 0)
        dve.wait_ge(chunk_done, n + 1 + CREDIT)
        nc.vector.tensor_scalar(halves(sq[0:SH]), acc[0:SH, (n % 2) * 4:(n % 2) * 4 + 2, 0:H], 1.0, None, ALU.mult
                                ).then_inc(epilogue_done, 1)
        chunks(dve, 8, lambda i, u: dve_rest(dve, base + 14, i, u))
        x, e, u1, ln = dtmp[:, 4], dtmp[:, 1], dtmp[:, 2], dtmp[:, 3]
        dve.wait_ge(conv_used, CREDIT + CONVS + 1)
        chain.link(nc.vector.memset(x, 0.0))
        dve.wait_ge(dt_turned, 1)
        nc.vector.tensor_copy(x[:, 0:4 * SH], acc[:, 7, 0:4 * SH]).then_inc(dve_side, 1)
        chain.link(nc.vector.tensor_copy(x[0:24, 4 * SH:5 * SH], acc[0:24, 7, 4 * SH:5 * SH]))
        x3 = x.rearrange("p (c h) -> p c h", h=SH)
        chain.link(nc.vector.tensor_tensor(x3, x3, headp[:, 0].unsqueeze(1).broadcast_to([P, 5, SH]), ALU.add))
        nc.vector.scalar_tensor_tensor(dtmp[:, 0], x, -1.0, x, ALU.mult, ALU.max).then_inc(dt_x, 1)
        dve.wait_ge(dt_e, 1)
        nc.vector.tensor_scalar(u1, e, 1.0, None, ALU.add).then_inc(dt_x, 1)
        dve.wait_ge(dt_x, 2)
        d, zero = dtmp[:, 0], dtmp[:, 5]
        chain.link(nc.vector.tensor_scalar(d, u1, 1.0, None, ALU.subtract))
        chain.link(nc.vector.tensor_scalar(zero, d, 0.0, None, ALU.is_equal))
        chain.link(nc.vector.tensor_tensor(d, d, zero, ALU.add))
        chain.link(nc.vector.reciprocal(d, d))
        dve.wait_ge(dt_e, 3)
        chain.link(nc.vector.tensor_tensor(ln, ln, d, ALU.mult))
        chain.link(nc.vector.tensor_tensor(ln, ln, zero, ALU.add))
        chain.link(nc.vector.tensor_tensor(ln, ln, e, ALU.mult))
        dtf = dtok[:].rearrange("p c h -> p (c h)")
        chain.link(nc.vector.scalar_tensor_tensor(dtf, x, 0.0, ln, ALU.max, ALU.add))
        nc.vector.scalar_tensor_tensor(dA[:], dtok[:], -1.0, headp[:, 1].unsqueeze(1).broadcast_to([P, 5, SH]),
                                       ALU.mult, ALU.mult).then_inc(dt_ready, 1)
        for c, m in SCHUNKS:
            dve.wait_ge(cum_done, c + 1)
            if c:
                dve.wait_ge(xd_ready, c)
            nc.vector.tensor_copy(cum[0:m, 0], acc[0:m, 5, 0:SH]).then_inc(dve_side, 1)
            chain.link(nc.vector.tensor_copy(cum[:, 1], acc[:, 5, SH:2 * SH]))
            nc.vector.tensor_tensor(decay[0:m], cum[0:m, 1], cum[0:m, 0], ALU.subtract).then_inc(cum_read, 1)
            dve.wait_ge(xturned, c + 1)
            nc.vector.tensor_tensor(xr[0:m], acc[0:m, 0:4, :].rearrange("p b (h d) -> p (b h) d", d=HD),
                                    dtok[0:m, c].unsqueeze(2).broadcast_to([m, SH, HD]), ALU.mult).then_inc(xr_ready, 1)
            if c:
                dve.wait_ge(st_done, SG * c)
            nc.vector.tensor_copy(Btok[0:m], acc[0:m, 4, :]).then_inc(xr_ready, 1)

            def arg(b):
                k = 8 * c + b
                dve.wait_ge(ec_ready, 8 * (c - 1) + b + 1) if c else dve.wait_ge(ab_done, k + 1)
                if k >= 2:
                    dve.wait_ge(y_done, k - 1)
                for i in range(4):
                    h = 4 * b + i
                    ins = nc.vector.tensor_scalar(Et[0:m, b % 2, i, 0:m], acc[0:m, 6 + b % 2, i * m:(i + 1) * m],
                                                  cum[0:m, 0, h:h + 1], 0.0, ALU.subtract, ALU.min)
                    ins.then_inc(arg_ready if i == 3 else dve_side, 1)

            def cb(g):
                dve.wait_ge(cb_done, SG * c + g + 1)
                if SG * c + g >= 2:
                    dve.wait_ge(m_ready, 2 * (SG * c + g - 1))
                nc.vector.tensor_tensor(CBm[0:m, g % 2, 0:m], acc[0:m, 4 + g % 2, 0:m], upto1[0:m, 0:m], ALU.mult
                                        ).then_inc(cb_ready, 1)

            def times_cb(b):
                k = 8 * c + b
                dve.wait_ge(e_ready, k + 1)
                dve.wait_ge(cb_ready, SG * c + b // 2 + 1)
                e4 = Et[0:m, b % 2, :, 0:m]
                nc.vector.tensor_tensor(e4, e4, CBm[0:m, b // 2 % 2, 0:m].unsqueeze(1).broadcast_to([m, 4, m]), ALU.mult
                                        ).then_inc(m_ready, 1)

            def outputs(g):
                dve.wait_ge(y_done, 8 * c + 2 * g + 2)
                for t in range(GAIN):
                    n = g * GAIN + t
                    xx = xbc[:, n, c * P:c * P + m]
                    ins = nc.vector.scalar_tensor_tensor(xx, xx, featp[:, 0, n:n + 1], acc[:, g % 2, t * P:t * P + m],
                                                         ALU.mult, ALU.add)
                    ins.then_inc(y_read if t == GAIN - 1 else dve_side, 1)
                dve.wait_ge(st_done, SG * c + g + 1)
                hg = hst[:, g * GEXP:(g + 1) * GEXP]
                st = acc[:, 2 + g % 2, :].rearrange("p (h d) -> p h d", d=HD)
                if c == 0:
                    nc.vector.tensor_copy(hg, st).then_inc(h_ready, 1)
                else:
                    dve.wait_ge(decay_ready, 2 * c + 1)
                    chain.link(nc.vector.tensor_tensor(hg, hg, cdecay[:, g * GEXP:(g + 1) * GEXP].unsqueeze(2).broadcast_to(
                        [P, GEXP, HD]), ALU.mult))
                    nc.vector.tensor_tensor(hg, hg, st, ALU.add).then_inc(h_ready, 1)

            for b in range(10):
                if b < 8:
                    if b % 2 == 0:
                        cb(b // 2)
                    arg(b)
                if 1 <= b <= 8:
                    times_cb(b - 1)
                if b >= 3 and b % 2 == 1:
                    outputs((b - 3) // 2)
        dve.wait_ge(sx_done, 1)
        chain.link(nc.vector.tensor_copy(dax, acc[:, 1, 0:XT * S].rearrange("p (t s) -> p t s", s=S)))
        nc.vector.tensor_tensor(dtx, acc[:, 0, 0:XT * S].rearrange("p (t s) -> p t s", s=S), xbc[:, 0:XT, T:N], ALU.mult
                                ).then_inc(sx_ready, 1)
        dve.wait_ge(sx_ready, 2)
        for s in range(S):
            e = s % 2
            dve.wait_ge(bc_done, s + 1)
            if s == 0:
                dve.wait_ge(ssd_out_done, 48)
            if s >= 2:
                dve.wait_ge(hs_reduced, s - 1)
            hp4 = hp[:, e].rearrange("p (g t) n -> p g t n", g=SG)
            for g in range(SG):
                ins = nc.vector.tensor_tensor(hp4[:, g], acc[:, 2 + e, g * P:(g + 1) * P].unsqueeze(1).broadcast_to([P, GAIN, P]),
                                              dtx[:, g * GAIN:(g + 1) * GAIN, s].unsqueeze(2).broadcast_to([P, GAIN, P]), ALU.mult)
                ins.then_inc(bx_ready if g == SG - 1 else dve_side, 1)
            dve.wait_ge(hs_ready, s + 1)
            for g in range(SG):
                ins = nc.vector.tensor_tensor(hp4[:, g], acc[:, 4 + e, g * P:(g + 1) * P].unsqueeze(1).broadcast_to([P, GAIN, P]),
                                              hs[:, e, g * GAIN:(g + 1) * GAIN, :], ALU.mult)
                ins.then_inc(hc_ready if g == SG - 1 else dve_side, 1)
            dve.wait_ge(hc_ready, s + 1)
            nc.vector.tensor_reduce(ysam[:, :, s], hp[:, e], AX.X, ALU.add).then_inc(hs_reduced, 1)
        xs = xbc[:, 0:XT, T:N]
        dve.wait_ge(hs_reduced, S)
        chain.link(nc.vector.tensor_tensor(xs, xs, featp[:, 0].unsqueeze(2).broadcast_to([P, XT, S]), ALU.mult))
        chain.link(nc.vector.tensor_tensor(xs, xs, ysam, ALU.add))
        dve.wait_ge(y_read, SG * 5)

        def gate(g):
            for t in range(g * GAIN, (g + 1) * GAIN):
                nc.vector.tensor_tensor(xbc[:, t], xbc[:, t], zT[:, t], ALU.mult).then_inc(gated, 1)

        gate(0)
        for g in range(SG):
            if g + 1 < SG:
                gate(g + 1)
            dve.wait_ge(gstd, g + 1)
            chain.link(nc.vector.reciprocal(rstd[:], rstd[:]))
            for t in range(g * GAIN, (g + 1) * GAIN):
                nc.vector.scalar_tensor_tensor(xbc[:, t], xbc[:, t], featp[:, 1, t:t + 1], rstd[:], ALU.mult, ALU.mult
                                               ).then_inc(yn_ready, 1)
        dve_residual(dve, "ssd_out", 1.0)

    def pool_ssd(pool, chain):
        for c, m in SCHUNKS:
            pool.wait_ge(decay_ready, 2 * c + 2)
            pool.wait_ge(xr_ready, 2 * c + 1)
            if c:
                pool.wait_ge(st_done, SG * c)
            nc.gpsimd.tensor_tensor(xd[0:m], xr[0:m], decay[0:m].unsqueeze(2).broadcast_to([m, SH, HD]), ALU.mult
                                    ).then_inc(xd_ready, 1)
            if c:
                for b in range(8):
                    pool.wait_ge(ec_ready, 8 * (c - 1) + b + 1)
                    c4 = Ct[:, b % 2, :, 0:m]
                    nc.gpsimd.tensor_tensor(c4, c4, xbc[:, BC + b // 2, c * P:c * P + m].unsqueeze(1).broadcast_to([P, 4, m]),
                                            ALU.mult).then_inc(cs_ready, 1)
        pool.wait_ge(sx_ready, 2)
        for s in range(S):
            e = s % 2
            pool.wait_ge(hs_loaded[e], 16 * (s // 2 + 1))
            chain.link(nc.gpsimd.tensor_tensor(hs[:, e], hs[:, e], dax[:, :, s].unsqueeze(2).broadcast_to([P, XT, P]), ALU.mult))
            pool.wait_ge(bx_ready, s + 1)
            nc.gpsimd.tensor_tensor(hs[:, e], hs[:, e], hp[:, e], ALU.add).then_inc(hs_ready, 1)
        for g in range(SG):
            for t in range(GAIN):
                n = g * GAIN + t
                pool.wait_ge(gsq, n + 1)
                if t == 0:
                    if g:
                        pool.wait_ge(gsum_done, g)
                    else:
                        pool.wait_ge(norm_sum_done, NORM["ssd"] + 1)
                    ins = nc.gpsimd.tensor_copy(ssum[:], sq[:])
                    ins.then_inc(gsum_step, 1)
                else:
                    pool.wait_ge(gsum_step, n)
                    nc.gpsimd.tensor_tensor(ssum[:], ssum[:], sq[:], ALU.add).then_inc(gsum_step, 1)
            pool.wait_ge(gsum_step, GAIN * (g + 1))
            nc.gpsimd.memset(credit[:, 0:1], 0.0).then_inc(gsum_ready, 1)
            for t in range(GAIN):
                n = g * GAIN + t
                pool.wait_ge(yh_ready, n + 1)
                nc.gpsimd.tensor_tensor(yl[:, n], xbc[:, n], yh[:, n].bitcast(F32), ALU.subtract).then_inc(yl_ready, 1)

    gsum_step, hs_reduced = sem("gsum_step"), sem("hs_reduced")
    swork = scrf[:, 0:CVT * S * 4].rearrange("p (t s j) -> p t s j", t=CVT, s=S)
    sconv = scrf[:, CVT * S * 4:CVT * S * 5].rearrange("p (t s) -> p t s", t=CVT)
    dtmp = scrf[:, 1152:1152 + 6 * 5 * SH].rearrange("p (a n) -> p a n", a=6)

    ffns = ["ffn0", "attn", "ffn1", "ffn2", "ssd", "ffn3"]
    order = ffns[:upto]

    def last(f):
        return order[-1] == f"ffn{f}"

    def ssum_after(n):
        what = order[n - 1]
        return {"attn": ("attn_out", 2), "ssd": ("ssd_out", 1)}.get(what) or (f"out{what[3]}1", 1)

    block = ctx.enter_context(nc.Block())

    @block.sync
    def _(sp):
        sp.dma_start(xT[:], I["xT"].rearrange("(t p) n -> p t n", p=P)).then_inc(x_loaded, 16)
        sp.dma_start(gains[:], I["gains"]).then_inc(consts_loaded, 16)
        sp.dma_start(headg[:], I["head_gains"]).then_inc(consts_loaded, 16)
        sp.dma_start(pages[:], I["page_table"].broadcast_to([P, S * NPG])).then_inc(consts_loaded, 16)
        sp.dma_start(vrow[:], I["page_of_lane"]).then_inc(consts_loaded, 16)
        sp.dma_start(lane[:], I["lane"]).then_inc(consts_loaded, 16)
        sp.wait_ge(consts_loaded, 80)
        for what in order:
            if what.startswith("ffn"):
                f = int(what[3])
                page = 0
                for g, kts in enumerate(GROUPS):
                    for section, source, width, start in (
                            (f"in{f}{g}", I["w_ffn_in"][f], BLK * P, sum(GROUPS[:g])),
                            (f"out{f}{g}", I[f"w_ffn_out{g}"][f], kts * P, 0)):
                        if f or page >= 14:
                            if f == 0:
                                for g2 in range(page, NPG):
                                    sp_index_pages(sp, g2)
                            sp_stream(sp, section, source, width, start)
                            continue
                        sp_stream(sp, section, source, width, start, lambda i: sp_index_pages(sp, i + page))
                        page += COUNT[section] // 2 - (1 if BASE[section] == 0 else 0)
            if what == "attn":
                sp_stream(sp, "attn_in", I["w_attn_in"], BLK * P)
                sp_out = I["w_attn_out"]
                base = BASE["attn_out"]
                for u in range(2):
                    sp.wait_ge(wl_ready, base + u - 1)
                    sp.dma_start(raw[:, (base + u) % 2], sp_out[u]).then_inc(w_loaded[(base + u) % 2], 16)
                sp_attention_outputs(sp)
                sp_keys(sp)
                for u in range(2, 4):
                    sp.wait_ge(wl_ready, base + u - 1)
                    sp.dma_start(raw[:, (base + u) % 2], sp_out[u]).then_inc(w_loaded[(base + u) % 2], 16)
            if what == "ssd":
                sp_ssd(sp)
        end = BASE["out%d1" % int(order[-1][3])] + DT + CREDIT
        sp.wait_ge(epilogue_done, end)
        sp.dma_start(O["yT"].rearrange("(t p) n -> p t n", p=P), xT[:]).then_inc(out_done, 16)
        sp.wait_ge(out_done, 16)
        sp.wait_ge(kv_out_done, 16 * 3)
        if "ssd" in order:
            sp.wait_ge(ssd_out_done, SSD_STORES * 16)

    @block.scalar
    def _(act):
        act_round(act, 0, 0, 0)
        act.wait_ge(consts_loaded, 80)
        for what in order:
            if what.startswith("ffn"):
                f = int(what[3])
                act_norm(act, NORM[what])
                for g in range(2):
                    act_ffn_in(act, f, g)
                    act_rounds(act, f"out{f}{g}", not (g == 1 and last(f)))
            if what == "attn":
                act_norm(act, NORM[what])
                act_rounds(act, "attn_in")
                act_attention(act)
                act_rounds(act, "attn_out")
            if what == "ssd":
                act_norm(act, NORM[what])
                act_ssd(act)

    @block.vector
    def _(dve):
        chain = Chain(dve, dve_chain)
        nc.vector.memset(ones[:], 1.0).then_inc(const_ready, 1)
        nc.vector.memset(epsc[:], EPS).then_inc(const_ready, 1)
        dve.wait_ge(x_loaded, 16)
        dve.wait_ge(consts_loaded, 80)
        dve.wait_ge(consts, 1)
        dve_rest(dve, 0, 0, 0)
        for what in order:
            if what.startswith("ffn"):
                f = int(what[3])
                dve_norm(dve, chain, NORM[what])
                for g in range(2):
                    dve_ffn_in(dve, f, g)
                    dve_residual(dve, f"out{f}{g}", 0.5, ahead=not (g == 1 and last(f)))
            if what == "attn":
                dve_norm(dve, chain, NORM[what])
                dve_copy_out(dve, "attn_in", hT, 8)
                dve_copy_out(dve, "attn_in", hT, 1, 8, 1)
                dve_attention(dve, chain)
                dve_residual(dve, "attn_out", 1.0, 2)
            if what == "ssd":
                dve_norm(dve, chain, NORM[what])
                dve_ssd(dve, chain)

    @block.gpsimd
    def _(pool):
        chain = Chain(pool, pool_chain)
        nc.gpsimd.memset(credit[:, 1:2], 0.0).then_inc(epilogue_done, CREDIT)
        nc.gpsimd.memset(credit[:, 2:3], 0.0).then_inc(g_ready, CREDIT)
        pool_consts(pool, chain)
        pool.wait_ge(const_ready, 1)
        pool_sumsq(pool, chain, 0)
        for n, what in enumerate(order):
            pool_norm(pool, NORM[what])
            if what.startswith("ffn"):
                f = int(what[3])
                for g in range(2):
                    pool_ffn_in(pool, chain, f, g)
            if what == "attn":
                pool_attention(pool)
            if what == "ssd":
                pool_ssd(pool, chain)
            if n + 1 < len(order):
                section, tiles = ssum_after(n + 1)
                pool_sumsq(pool, chain, n + 1, section, tiles)

    @block.tensor
    def _(pe):
        pe.wait_ge(const_ready, 2)
        pe.wait_ge(consts, 1)
        for what in order:
            if what.startswith("ffn"):
                f = int(what[3])
                pe_ffn(pe, f, NORM[what])
            if what == "attn":
                k = NORM[what]
                pe_norm(pe, k)

                def normed(kt):
                    pe.wait_ge(xl_ready, DT * k + kt + 1)

                pe_pairs(pe, "attn_in", normed, 0, 8)
                pe_pairs(pe, "attn_in", normed, 8, 1, 1)
                pe_attention(pe)
                pe_pairs(pe, "attn_out", lambda kt: pe.wait_ge(at_xl, kt + 1))
            if what == "ssd":
                pe_norm(pe, NORM[what])
                pe_ssd(pe)

    ctx.close()


def lay_out(inputs):
    a = {k: np.asarray(v) for k, v in inputs.items()}
    L = {}
    L["xT"] = np.concatenate([a["meta_tokens"], a["x_prompt"][0], a["x_sample"][:, 0]]).T
    g = [a["norm_ffn_a"][0], a["norm_mix"][0], a["norm_ffn_b"][0], a["norm_ffn_a"][1], a["norm_mix"][1],
         a["norm_ffn_b"][1]]
    L["gains"] = np.stack(g).reshape(6, DT, P).transpose(2, 0, 1)
    w_in = np.stack([a["w_ffn_a_in"][0], a["w_ffn_b_in"][0], a["w_ffn_a_in"][1], a["w_ffn_b_in"][1]])
    L["w_ffn_in"] = w_in.reshape(4, DT, P, 2, FT, P).transpose(0, 4, 2, 1, 3, 5).reshape(4, FT, P, BLK * P)
    w_out = np.stack([a["w_ffn_a_out"][0], a["w_ffn_b_out"][0], a["w_ffn_a_out"][1], a["w_ffn_b_out"][1]])
    w_out = w_out.reshape(4, FT, P, DT, P).transpose(0, 3, 2, 1, 4)
    for n, (start, kts) in enumerate(((0, GROUPS[0]), (GROUPS[0], GROUPS[1]))):
        L[f"w_ffn_out{n}"] = w_out[:, :, :, start:start + kts].reshape(4, DT, P, kts * P)
    lay_out_attention(a, L)
    lay_out_ssd(a, L)
    return {k: np.ascontiguousarray(v) for k, v in L.items()}


def lay_out_attention(a, L):
    heads = a["w_attn_in"][0]
    q = heads[:, :D].reshape(D, 2, 2, REP, HD).transpose(0, 1, 3, 2, 4).reshape(D, D)
    rest = heads[:, D:]
    cols = np.concatenate([q, rest, np.zeros((D, 18 * P - D - rest.shape[1]), np.float32)], axis=1)
    L["w_attn_in"] = pair_chunks(cols)
    w_out = a["w_attn_out"][0].reshape(2, 2, REP, HD, D).transpose(0, 2, 1, 3, 4).reshape(D, D)
    L["w_attn_out"] = pair_chunks(w_out)
    gq, gk, gi = a["q_norm"][0], a["k_norm"][0], a["kidx_norm"][0]
    z = np.zeros(P, np.float32)
    L["head_gains"] = np.stack([np.tile(gq, 2), np.tile(gk, 2), np.tile(gi, 2), z], axis=1)
    L["page_table"] = a["page_table"].reshape(1, S * NPG)
    L["page_of_lane"] = np.repeat(a["page_table"].T, P // NPG, axis=0)
    L["lane"] = np.stack([np.arange(P), np.arange(P) % (P // NPG)], axis=1).astype(np.int32)
    L["kidx"] = a["cache_kidx"][0].transpose(0, 2, 1)
    L["kpages"] = a["cache_k"][0].reshape(POOL, PAGE, 2, P).transpose(0, 3, 1, 2).reshape(POOL, P, 2 * PAGE)
    L["vpages"] = a["cache_v"][0].reshape(POOL, PAGE, NKV * HD)


def pair_chunks(w):
    n = w.shape[1] // (2 * P)
    return w.reshape(DT, P, n, 2, P).transpose(2, 1, 0, 3, 4).reshape(n, P, BLK * P)


def lay_out_ssd(a, L):
    w = a["w_ssd_in"][0]
    z, xbc, dt = w[:, :DI], w[:, DI:DI + CVT * P], w[:, DI + CVT * P:]
    L["w_ssd_in"] = pair_chunks(np.concatenate([xbc, dt, np.zeros((D, 2 * P - SH), np.float32), z], axis=1))
    w_out = a["w_ssd_out"][0].reshape(XT, P, DT, P)
    L["w_ssd_out"] = w_out.transpose(2, 1, 0, 3).reshape(DT, P, XT * P)
    L["conv_w"] = a["conv_w"][0].reshape(4, CVT, P).transpose(2, 1, 0).reshape(P, CVT * 4)
    L["conv_b"] = a["conv_b"][0].reshape(CVT, P).T
    past = a["state_conv"][0].reshape(S, 3, CVT, P).transpose(3, 2, 0, 1)
    L["state_conv"] = np.concatenate([past, np.zeros((P, CVT, S, 1), np.float32)], axis=3).reshape(P, CVT * S * 4)
    d_skip = np.repeat(a["d_skip"][0], HD).reshape(XT, P)
    gate = a["gate_norm"][0].reshape(XT, P)
    L["feature_params"] = np.stack([d_skip, gate]).transpose(2, 0, 1).reshape(P, 2 * XT)
    L["head_params"] = np.concatenate([a["dt_bias"][0], a["a_log"][0]]).reshape(1, 2 * SH)
    L["state_ssm"] = a["state_ssm"][0].reshape(S, XT, P, P).transpose(0, 2, 1, 3)


OUT_SHAPES = {"yT": (D, N), "kT": (NKV * HD, N), "vT": (NKV * HD, N), "kiT": (HD, N), "hT": (P, DI),
              "hs": (S, P, XT, P), "conv_prompt": (P, CVT * 3), "conv_sample": (P, CVT * S * 4)}


def take_apart(r):
    y = r["yT"].T
    k, v, ki = (r[n].T for n in ("kT", "vT", "kiT"))
    heads = (NKV, HD)
    convp = r["conv_prompt"].reshape(P, CVT, 3).transpose(2, 1, 0).reshape(1, 1, 3, CVT * P)
    convs = r["conv_sample"].reshape(P, CVT, S, 4)[..., 1:].transpose(2, 3, 1, 0).reshape(1, S, 3, CVT * P)
    hp = r["hT"].reshape(P, SH, HD).transpose(1, 2, 0).reshape(1, 1, SH, HD, P)
    hs = r["hs"].transpose(0, 2, 1, 3).reshape(1, S, SH, HD, P)
    out = (y[META:T].reshape(1, SEQ, D), y[T:].reshape(S, 1, D),
           k[:T].reshape((1, 1, T) + heads), v[:T].reshape((1, 1, T) + heads), ki[:T].reshape(1, 1, T, HD),
           k[T:].reshape((1, S, 1) + heads), v[T:].reshape((1, S, 1) + heads), ki[T:].reshape(1, S, 1, HD),
           hp, convp, hs, convs)
    return tuple(np.ascontiguousarray(o) for o in out)


def kernel(**inputs):
    import concourse.bacc as bacc
    from concourse.bass_utils import run_bass_kernel_spmd

    nc = bacc.Bacc("TRN2", target_bir_lowering=False, num_devices=1)
    arrays = {"in_" + k: v for k, v in lay_out(inputs).items()}
    ins = {k[3:]: nc.dram_tensor(k, v.shape, mybir.dt.from_np(v.dtype), kind="ExternalInput").ap() for k, v in arrays.items()}
    outs = {k: nc.dram_tensor("out_" + k, shape, F32, kind="ExternalOutput").ap() for k, shape in OUT_SHAPES.items()}
    build(nc, ins, outs)
    r = run_bass_kernel_spmd(nc, [arrays], core_ids=[0]).results[0]
    return take_apart({k: r["out_" + k] for k in OUT_SHAPES})
```
